# Optimizing a Trainium2 kernel written in Bass

```python
import math
import jax, jax.numpy as jnp
from jax import lax
import numpy as np

D_MODEL = 1024
BATCH = 1
SEQ = 1024
DEPTH = 1

N_MIXERS = 4
EPS = 1e-6

SB_HEADS = 16
SB_HEAD_DIM = D_MODEL // SB_HEADS
SB_WIDTH = SB_HEADS * SB_HEAD_DIM
SB_BLOCK = 128

HG_HEAD_DIM = 128
HG_WIDTH = D_MODEL
HG_HEADS = HG_WIDTH // HG_HEAD_DIM
HG_CHUNK = 64

M2_WIDTH = 2 * D_MODEL
M2_HEAD_DIM = 64
M2_HEADS = M2_WIDTH // M2_HEAD_DIM
M2_GROUPS = 8
M2_STATE = 128
M2_CONV = 4
M2_CHUNK = 128
M2_CONV_DIM = M2_WIDTH + 2 * M2_GROUPS * M2_STATE
M2_IN = M2_WIDTH + M2_CONV_DIM + M2_HEADS

RET_HEADS = 4
RET_QK_DIM = D_MODEL // RET_HEADS
RET_V_WIDTH = 2 * D_MODEL
RET_V_DIM = RET_V_WIDTH // RET_HEADS
RET_CHUNK = 128
RET_ROT_BASE = 10000.0
RET_IN = 2 * D_MODEL + 2 * RET_V_WIDTH

kernel_name = "hybrid_interleaved_sb_hgrn2_ssd_retention"

F32 = jnp.float32

def _rms(x, eps=EPS):
    xf = x.astype(F32)
    return xf * lax.rsqrt(jnp.mean(xf * xf, axis=-1, keepdims=True) + eps)

def rmsnorm(x, g):
    return (_rms(x) * g.astype(F32)).astype(x.dtype)

def _layers_of(m):
    return len(range(m, DEPTH, N_MIXERS))

def stick_breaking_attention(q, k, v):
    b, h, s, d = q.shape
    nb = s // SB_BLOCK
    scale = d ** -0.5
    kf = k.astype(F32)
    vf = v.astype(F32)
    key_pos = jnp.arange(s)
    q_blocks = q.reshape(b, h, nb, SB_BLOCK, d).transpose(2, 0, 1, 3, 4)

    def one_block(args):
        qb, blk = args
        q_pos = blk * SB_BLOCK + jnp.arange(SB_BLOCK)
        mask = key_pos[None, :] < q_pos[:, None]
        z = jnp.einsum('bhqd,bhkd->bhqk', qb.astype(F32), kf) * scale
        log_beta = jax.nn.log_sigmoid(z)
        log_1m = jnp.where(mask, log_beta - z, 0.0)
        after = lax.cumsum(log_1m, axis=3, reverse=True) - log_1m
        a = jnp.where(mask, jnp.exp(log_beta + after), 0.0)
        return jnp.einsum('bhqk,bhkd->bhqd', a, vf)

    out = lax.map(one_block, (q_blocks, jnp.arange(nb)))
    return out.transpose(1, 2, 0, 3, 4).reshape(b, h, s, d)

def sb_mixer(h, w_in, w_out):
    b, s, _ = h.shape
    q, k, v, gate = jnp.split(h @ w_in, 4, axis=-1)
    heads = lambda t: t.reshape(b, s, SB_HEADS, SB_HEAD_DIM).transpose(0, 2, 1, 3)
    o = stick_breaking_attention(heads(q), heads(k), heads(v))
    o = o.transpose(0, 2, 1, 3).reshape(b, s, SB_WIDTH)
    return (o * jax.nn.silu(gate.astype(F32))) @ w_out

def hgrn2_mixer(h, w_in, lb, norm_g, w_out):
    b, s, _ = h.shape
    C = HG_CHUNK
    nc = s // C
    q, f_pre, i, gate = jnp.split(h @ w_in, 4, axis=-1)
    q = jax.nn.silu(q.astype(F32))
    f = lb + (1.0 - lb) * jax.nn.sigmoid(f_pre.astype(F32))
    log_f = jnp.log(f)
    k = 1.0 - f

    def chunks(t):
        return t.astype(F32).reshape(b, nc, C, HG_HEADS, HG_HEAD_DIM).transpose(1, 0, 3, 2, 4)

    tri = jnp.tril(jnp.ones((C, C), dtype=bool))[:, :, None]

    def step(state, inp):
        qb, kb, vb, gb = inp
        cum = jnp.cumsum(gb, axis=2)
        diff = cum[:, :, :, None, :] - cum[:, :, None, :, :]
        decay = jnp.exp(jnp.where(tri, diff, -jnp.inf))
        scores = jnp.einsum('bhtd,bhsd,bhtsd->bhts', qb, kb, decay)
        o = jnp.einsum('bhts,bhsv->bhtv', scores, vb) \
            + jnp.einsum('bhtd,bhdv->bhtv', qb * jnp.exp(cum), state)
        last = cum[:, :, -1:, :]
        new_state = jnp.exp(last[:, :, 0, :, None]) * state \
            + jnp.einsum('bhsd,bhsv->bhdv', kb * jnp.exp(last - cum), vb)
        return new_state, o

    init = jnp.zeros((b, HG_HEADS, HG_HEAD_DIM, HG_HEAD_DIM), F32)
    _, o = lax.scan(step, init, (chunks(q), chunks(k), chunks(i), chunks(log_f)))
    o = o.transpose(1, 0, 3, 2, 4).reshape(b, s, HG_HEADS, HG_HEAD_DIM)
    o = _rms(o) * norm_g.reshape(HG_HEADS, HG_HEAD_DIM).astype(F32)
    o = o.reshape(b, s, HG_WIDTH)
    return (o * jax.nn.silu(gate.astype(F32))) @ w_out

def causal_depthwise_conv(x, w, bias):
    ch = x.shape[-1]
    y = lax.conv_general_dilated(
        x, w[:, None, :].astype(x.dtype), window_strides=(1,),
        padding=[(w.shape[0] - 1, 0)], dimension_numbers=('NWC', 'WIO', 'NWC'),
        feature_group_count=ch)
    return y + bias

def ssd_scan(x, a_dt, bm, cm):
    b, s, H, P = x.shape
    G, N = bm.shape[2], bm.shape[3]
    R = H // G
    L = M2_CHUNK
    nc = s // L
    x = x.astype(F32).reshape(b, nc, L, G, R, P)
    a = a_dt.reshape(b, nc, L, G, R).transpose(0, 1, 3, 4, 2)
    bm = bm.astype(F32).reshape(b, nc, L, G, N)
    cm = cm.astype(F32).reshape(b, nc, L, G, N)
    a_cum = jnp.cumsum(a, axis=-1)
    tri = jnp.tril(jnp.ones((L, L), dtype=bool))
    seg = a_cum[..., :, None] - a_cum[..., None, :]
    decay = jnp.exp(jnp.where(tri, seg, -jnp.inf))
    cb = jnp.einsum('bclgn,bcsgn->bcgls', cm, bm)
    y_diag = jnp.einsum('bcgls,bcgrls,bcsgrp->bclgrp', cb, decay, x)
    decay_to_end = jnp.exp(a_cum[..., -1:] - a_cum)
    chunk_states = jnp.einsum('bclgn,bcgrl,bclgrp->bcgrpn', bm, decay_to_end, x)
    chunk_decay = jnp.exp(a_cum[..., -1])

    def step(state, inp):
        st, dec = inp
        return dec[..., None, None] * state + st, state

    init = jnp.zeros((b, G, R, P, N), F32)
    _, prev = lax.scan(step, init, (jnp.moveaxis(chunk_states, 1, 0), jnp.moveaxis(chunk_decay, 1, 0)))
    prev = jnp.moveaxis(prev, 0, 1)
    y_off = jnp.einsum('bclgn,bcgrpn,bcgrl->bclgrp', cm, prev, jnp.exp(a_cum))
    return (y_diag + y_off).reshape(b, s, H, P)

def mamba2_mixer(h, w_in, conv_w, conv_b, dt_bias, a_log, d_skip, norm_g, w_out):
    b, s, _ = h.shape
    z, xbc, dt = jnp.split(h @ w_in, [M2_WIDTH, M2_WIDTH + M2_CONV_DIM], axis=-1)
    xbc = jax.nn.silu(causal_depthwise_conv(xbc, conv_w, conv_b))
    xs, bm, cm = jnp.split(xbc, [M2_WIDTH, M2_WIDTH + M2_GROUPS * M2_STATE], axis=-1)
    dt = jax.nn.softplus(dt.astype(F32) + dt_bias.astype(F32))
    a = -jnp.exp(a_log.astype(F32))
    xh = xs.astype(F32).reshape(b, s, M2_HEADS, M2_HEAD_DIM)
    y = ssd_scan(xh * dt[..., None], dt * a,
                 bm.reshape(b, s, M2_GROUPS, M2_STATE), cm.reshape(b, s, M2_GROUPS, M2_STATE))
    y = y + d_skip.astype(F32)[:, None] * xh
    y = y.reshape(b, s, M2_WIDTH) * jax.nn.silu(z.astype(F32))
    gs = M2_WIDTH // M2_GROUPS
    y = (_rms(y.reshape(b, s, M2_GROUPS, gs)) * norm_g.reshape(M2_GROUPS, gs).astype(F32)).reshape(b, s, M2_WIDTH)
    return y @ w_out

def theta_rotate(x):
    b, s, H, d = x.shape
    angle = 1.0 / (RET_ROT_BASE ** jnp.linspace(0.0, 1.0, d // 2, dtype=F32))
    ph = jnp.arange(s, dtype=F32)[:, None] * angle[None, :]
    cos, sin = jnp.cos(ph)[None, :, None, :], jnp.sin(ph)[None, :, None, :]
    xp = x.astype(F32).reshape(b, s, H, d // 2, 2)
    x0, x1 = xp[..., 0], xp[..., 1]
    return jnp.stack([x0 * cos - x1 * sin, x1 * cos + x0 * sin], axis=-1).reshape(b, s, H, d)

def chunk_retention(q, k, v):
    b, s, H, dk = q.shape
    dv = v.shape[-1]
    C = RET_CHUNK
    nc = s // C
    log_g = jnp.log1p(-jnp.exp2(-5.0 - jnp.arange(H, dtype=F32)))
    qc = q.reshape(b, nc, C, H, dk)
    kc = k.reshape(b, nc, C, H, dk)
    vc = v.astype(F32).reshape(b, nc, C, H, dv)
    idx = jnp.arange(C, dtype=F32)
    rel = idx[:, None] - idx[None, :]
    intra = jnp.where(rel >= 0, jnp.exp(log_g[:, None, None] * jnp.maximum(rel, 0.0)), 0.0)
    scores = jnp.einsum('bcthd,bcshd->bchts', qc, kc) * intra
    o_intra = jnp.einsum('bchts,bcshv->bcthv', scores, vc)
    k_decay = jnp.exp(log_g[:, None] * (C - 1.0 - idx))
    chunk_states = jnp.einsum('bcshd,hs,bcshv->bchdv', kc, k_decay, vc)
    chunk_decay = jnp.exp(log_g * C)[:, None, None]

    def step(state, st):
        return chunk_decay * state + st, state

    init = jnp.zeros((b, H, dk, dv), F32)
    _, prev = lax.scan(step, init, jnp.moveaxis(chunk_states, 1, 0))
    prev = jnp.moveaxis(prev, 0, 1)
    q_decay = jnp.exp(log_g[:, None] * (idx + 1.0))
    o_inter = jnp.einsum('bcthd,ht,bchdv->bcthv', qc, q_decay, prev)
    return (o_intra + o_inter).reshape(b, s, H, dv)

def retention_mixer(h, w_in, w_out):
    b, s, _ = h.shape
    q, k, v, gate = jnp.split(h @ w_in, [D_MODEL, 2 * D_MODEL, 2 * D_MODEL + RET_V_WIDTH], axis=-1)
    q = theta_rotate(q.reshape(b, s, RET_HEADS, RET_QK_DIM))
    k = theta_rotate(k.reshape(b, s, RET_HEADS, RET_QK_DIM)) * (RET_QK_DIM ** -0.5)
    o = chunk_retention(q, k, v.reshape(b, s, RET_HEADS, RET_V_DIM))
    o = _rms(o).reshape(b, s, RET_V_WIDTH)
    return (o * jax.nn.silu(gate.astype(F32))) @ w_out

def setup_inputs(seed: int = 0) -> dict:
    key = jax.random.key(seed)
    ks = jax.random.split(key, 24)
    nA, nB, nC, nD = (_layers_of(m) for m in range(N_MIXERS))

    def w(k, shape, fan_in):
        return jax.random.normal(k, shape, F32) * (fan_in ** -0.5)

    def gain(k, shape):
        return 1.0 + 0.02 * jax.random.normal(k, shape, F32)

    dt0 = jnp.exp(jax.random.uniform(ks[12], (nC, M2_HEADS), F32, math.log(1e-3), math.log(1e-1)))
    return {
        "x": jax.random.normal(ks[0], (BATCH, SEQ, D_MODEL), F32),
        "norm_g": gain(ks[1], (DEPTH, D_MODEL)),
        "sb_w_in": w(ks[2], (nA, D_MODEL, 4 * SB_WIDTH), D_MODEL),
        "sb_w_out": w(ks[3], (nA, SB_WIDTH, D_MODEL), SB_WIDTH),
        "hg_w_in": w(ks[4], (nB, D_MODEL, 4 * HG_WIDTH), D_MODEL),
        "hg_lb_logits": 0.5 * jax.random.normal(ks[5], (DEPTH, HG_WIDTH), F32),
        "hg_norm_g": gain(ks[6], (nB, HG_WIDTH)),
        "hg_w_out": w(ks[7], (nB, HG_WIDTH, D_MODEL), HG_WIDTH),
        "m2_w_in": w(ks[8], (nC, D_MODEL, M2_IN), D_MODEL),
        "m2_conv_w": w(ks[9], (nC, M2_CONV, M2_CONV_DIM), M2_CONV),
        "m2_conv_b": 0.02 * jax.random.normal(ks[10], (nC, M2_CONV_DIM), F32),
        "m2_dt_bias": dt0 + jnp.log(-jnp.expm1(-dt0)),
        "m2_a_log": jnp.log(jax.random.uniform(ks[13], (nC, M2_HEADS), F32, 1.0, 16.0)),
        "m2_d": gain(ks[14], (nC, M2_HEADS)),
        "m2_norm_g": gain(ks[15], (nC, M2_WIDTH)),
        "m2_w_out": w(ks[16], (nC, M2_WIDTH, D_MODEL), M2_WIDTH),
        "ret_w_in": w(ks[17], (nD, D_MODEL, RET_IN), D_MODEL),
        "ret_w_out": w(ks[18], (nD, RET_V_WIDTH, D_MODEL), RET_V_WIDTH),
        "final_g": gain(ks[19], (D_MODEL,)),
    }

def reference(x, norm_g, sb_w_in, sb_w_out, hg_w_in, hg_lb_logits, hg_norm_g, hg_w_out,
              m2_w_in, m2_conv_w, m2_conv_b, m2_dt_bias, m2_a_log, m2_d, m2_norm_g, m2_w_out,
              ret_w_in, ret_w_out, final_g):
    lb_cum = jnp.cumsum(jax.nn.softmax(hg_lb_logits.astype(F32), axis=0), axis=0)
    lower_bounds = lb_cum - lb_cum[0]
    for i in range(DEPTH):
        m, j = i % N_MIXERS, i // N_MIXERS
        h = rmsnorm(x, norm_g[i])
        if m == 0:
            y = sb_mixer(h, sb_w_in[j], sb_w_out[j])
        elif m == 1:
            y = hgrn2_mixer(h, hg_w_in[j], lower_bounds[i], hg_norm_g[j], hg_w_out[j])
        elif m == 2:
            y = mamba2_mixer(h, m2_w_in[j], m2_conv_w[j], m2_conv_b[j], m2_dt_bias[j],
                             m2_a_log[j], m2_d[j], m2_norm_g[j], m2_w_out[j])
        else:
            y = retention_mixer(h, ret_w_in[j], ret_w_out[j])
        x = x + y.astype(x.dtype)
    return rmsnorm(x, final_g)


_drawn_inputs = setup_inputs


def setup_inputs(seed=0):
    import zlib

    import numpy as np

    out = dict(_drawn_inputs(seed))
    spreads = {}
    factors = {'norm_g': 4.656, 'final_g': 2.838}
    for name, (base, spread) in spreads.items():
        noise = np.random.default_rng([zlib.crc32(name.encode()), seed]).standard_normal(out[name].shape)
        drawn = base * np.exp(spread * noise) if base else spread * noise
        out[name] = __import__('jax').numpy.asarray(drawn.astype(out[name].dtype))
    for name, factor in factors.items():
        out[name] = (out[name] * factor).astype(out[name].dtype)
    return out
```

```python
from contextlib import ExitStack

import concourse.bass as bass
from concourse import mybir

ALU = mybir.AluOpType
ACT = mybir.ActivationFunctionType
F32 = mybir.dt.float32
F32R = mybir.dt.float32r
BF16 = mybir.dt.bfloat16

P = 128
D = 1024
S = 1024
HEADS = 16
HD = D // HEADS
PAIRS = HEADS // 2
KB = D // P
HALF = 512
GQ = HALF // P
SLOTS = 16
EPS = 1e-6
MASKED = -1e30
SCALE = HD ** -0.5

UNITS0 = 3
T_PER_PAIR, AV_PER_PAIR = 26, 24


def plan(with_v):
    out, t, av = [], 0, 0
    for s in range(SLOTS):
        v_t = None
        if with_v and s in (6, 8):
            v_t, t = t, t + 1
        hh, grp = ((1, 1), (0, 0), (0, 1), (1, 0))[s // 4]
        blocks = (2 * (s % 4), 2 * (s % 4) + 1) if grp else (s % 4,)
        units = []
        for j in blocks:
            units.append((t, av, hh, grp, j))
            t, av = t + 1, av + 1
        out.append((v_t, units))
    return out


STEADY, LAST = plan(True), plan(False)
FIRST_SKIPS = 8


def t_base(p):
    if isinstance(p, int) and p == PAIRS:
        return t_base(PAIRS - 1) + T_PER_PAIR - 2
    return T_PER_PAIR * p + (2 - FIRST_SKIPS)


def av_base(p):
    return AV_PER_PAIR * p - FIRST_SKIPS


def is_last(p):
    return isinstance(p, int) and p == PAIRS - 1


def is_tail(p):
    return isinstance(p, int) and p == PAIRS


def is_first(p):
    return isinstance(p, int) and p == 0


def wait(eng, sem, value):
    if not isinstance(value, int) or value > 0:
        eng.wait_ge(sem, value)


def units_at(p, s):
    if isinstance(p, int) and (p == 0 and s < 4 or p == PAIRS and s >= 4):
        return []
    return (LAST if isinstance(p, int) and p >= PAIRS - 1 else STEADY)[s][1]


def av_at(p, s):
    if s > 0:
        return units_at(p, s - 1)
    return [] if is_first(p) else [(-1, -1, 1, 0, GQ - 1)]


def v_t_at(p, s):
    return None if isinstance(p, int) and p >= PAIRS - 1 else STEADY[s][0]


def proj_slots(p):
    return range(4) if is_last(p) else range(SLOTS)


def kind_of(p, s):
    return "g" if is_last(p) else "kvqg"[s // 4]


def evac_at(p, s):
    if s % 2 or is_tail(p) or (is_first(p) and s == 0):
        return None
    number = 2 * UNITS0 + 8 * p + s // 2 - 1
    if s == 0:
        return "g", 1, number
    return (kind_of(p, s - 1), ((s - 1) % 4) // 2, number) if (s - 1) in proj_slots(p) else None


def gate_at(p, s):
    evac = evac_at(p, s)
    if is_last(p) and s == 6:
        return 1, 2 * p + 1
    if not evac or evac[0] != "g" or (is_last(p) and s == 4):
        return None
    return evac[1], 2 * p - 1 if s == 0 else 2 * p + evac[1]


PROLOGUE = (("k", 0), ("v", 0), ("k", 1), ("v", 1), ("q", 0), ("q", 1))
EARLY_TILES = 5
EARLY = [(n, b) for n in range(EARLY_TILES) for b in range(PAIRS - 1)]
EARLY_BY_SLOT = {(PAIRS - 1, 12): 2, (PAIRS - 1, 13): 2, (PAIRS - 1, 14): 2, (PAIRS - 1, 15): 1}
EARLY_BY_SLOT |= {(PAIRS, s): 4 for s in range(5)}


def stick_breaking_layer(nc, x, norm_g, w_in, w_out, final_g, out):
    o_hi_dram = nc.dram_tensor("o_hi_scratch", [PAIRS, P, S], F32).ap()
    o_lo_dram = nc.dram_tensor("o_lo_scratch", [PAIRS, P, S], F32).ap()

    with ExitStack() as ctx:
        def sb(name, shape, dt=F32):
            return ctx.enter_context(nc.sbuf_tensor(name, shape, dt))

        def ps(name, shape, dt=F32):
            return ctx.enter_context(nc.psum_tensor(name, shape, dt))

        def sem(name):
            return ctx.enter_context(nc.semaphore(name))

        hT = sb("hT", [P, 2, KB, S], F32R)
        arena = sb("arena", [P, 2, 4, 2 * S], F32R)
        w_split = sb("w_split", [P, 2, 2, KB, P], F32R)
        w_raw = sb("w_raw", [P, 2, HALF])
        a_g = [sb("a_group0", [P, GQ, HALF]), sb("a_group1", [P, GQ, S])]
        rest = sb("rest", [P, 2, S + 1])
        aT = sb("aT", [P, 2, 2, HALF], F32R)
        aT_pad = sb("aT_pad", [P, 2, 2 * P], F32R)
        stage = sb("stage", [P, 2, HALF])
        gate = sb("gate", [P, S])
        oT = sb("oT", [P, S])
        o_split = sb("o_split", [P, 2, HALF], F32R)
        ident = sb("ident", [P, P])
        ident_bf = sb("ident_bf", [P, P], BF16)
        mask_bf = sb("mask_bf", [P, P], BF16)
        g_col = sb("g_col", [P, KB])
        ssq = sb("ssq", [P, 2 * KB])
        rstd = sb("rstd", [P, KB])
        mean_sq = sb("mean_sq", [P, KB])
        newton = sb("newton", [P, KB])
        eps_col = sb("eps_col", [P, 1])

        x_blocks = ([a_g[1][:, b, :] for b in range(4)]
                    + [a_g[0][:, 2 * b:2 * b + 2, :].rearrange("p a n -> p (a n)") for b in range(2)]
                    + [rest[:, b, 0:S] for b in range(2)])

        def q_of(par, hh):
            return arena[:, par, 0, hh * S:(hh + 1) * S]

        def k_of(par, hh, swapped):
            return arena[:, par, 2 if swapped else 1, hh * S:(hh + 1) * S]

        def v_of(par):
            return arena[:, par, 3, :].rearrange("p (b x d) -> p b x d", b=KB, x=4)

        def w_out_of(half, hl):
            return arena[:, half, 2 * hl:2 * hl + 2, :].rearrange("p a (b n) -> p (a b) n", n=HALF)

        z_ps = [ps(f"z_ps{b}", [P, S]) for b in range(2)]
        t_ps = [ps(f"t_ps{b}", [P, HALF]) for b in range(2)]
        proj_ps = ps("proj_ps", [P, HALF])
        o_ps = ps("o_ps", [P, HALF])
        y_banks = [proj_ps] + [z[:, c:c + HALF] for z in z_ps for c in (0, HALF)]
        four_banks = y_banks[1:]

        x_loaded = [sem(f"x_loaded{b}") for b in range(KB)]
        g_loaded = sem("g_loaded")
        consts_ready = sem("consts_ready")
        x_squared = sem("x_squared")
        mean_ready = sem("mean_ready")
        root_ready = sem("root_ready")
        rstd_ready = sem("rstd_ready")
        x_scaled = sem("x_scaled")
        xt_done = sem("xt_done")
        xt_hi = sem("xt_hi")
        xt_lo = sem("xt_lo")
        w_loaded = [sem(f"w_loaded{b}") for b in range(2)]
        w_hi = sem("w_hi")
        w_ready = sem("w_ready")
        proj_done = sem("proj_done")
        stage_ready = sem("stage_ready")
        qk_hi = sem("qk_hi")
        qk_split = sem("qk_split")
        gate_sig = sem("gate_sig")
        gate_ready = sem("gate_ready")
        k_swapped = sem("k_swapped")
        z_ready = sem("z_ready")
        rest_ready = sem("rest_ready")
        beta_ready = sem("beta_ready")
        scan_done = sem("scan_done")
        a_ready = sem("a_ready")
        t_done = sem("t_done")
        t_hi = sem("t_hi")
        t_lo = sem("t_lo")
        av_done = sem("av_done")
        o_shift = sem("o_shift")
        o_summed = sem("o_summed")
        o_gated = sem("o_gated")
        o_hi = sem("o_hi")
        o_lo = sem("o_lo")
        o_stored = sem("o_stored")
        o_loaded = [sem(f"o_loaded{b}") for b in range(PAIRS - 1)]
        wo_loaded = [sem(f"wo_loaded{b}") for b in range(2)]
        wo_hi = sem("wo_hi")
        wo_ready = sem("wo_ready")
        y_done = sem("y_done")
        y_sum = sem("y_sum")
        y_squared = sem("y_squared")
        ssq_summed = sem("ssq_summed")
        zeros_ready = sem("zeros_ready")
        xr_loaded = [sem(f"xr_loaded{b}") for b in range(4)]
        fg_loaded = sem("fg_loaded")
        out_ready = sem("out_ready")
        stored = [sem(f"stored{b}") for b in range(2)]
        table_loaded = sem("table_loaded")
        x_squared_dve = sem("x_squared_dve")

        block = ctx.enter_context(nc.Block())

        y_half = a_g[1][:, :, :].rearrange("p a (b n) -> p (a b) n", b=2)

        def y_of(n):
            return y_half[:, n, :] if n < KB else gate[:, (n % 2) * HALF:(n % 2 + 1) * HALF]

        def out_of(b):
            return [stage[:, 0, :], stage[:, 1, :]] if b % 2 else [oT[:, 0:HALF], oT[:, HALF:S]]

        def split_of(p, half):
            if is_tail(p):
                cols = slice(half * HALF, (half + 1) * HALF)
                return hT[:, 0, PAIRS - 1, cols], hT[:, 1, PAIRS - 1, cols]
            return o_split[:, 0, :], o_split[:, 1, :]

        def load_x_block(eng, b):
            eng.dma_start(x_blocks[b], x[b * P:(b + 1) * P, :]).then_inc(x_loaded[b], 16)

        def over_pairs(eng, slot, last_slot=6):
            for s in range(SLOTS):
                slot(0, 0, s)
            with eng.Fori(0, (PAIRS - 2) // 2) as two:
                for odd in range(2):
                    for s in range(SLOTS):
                        slot(two * 2 + (1 + odd), 1 - odd, s)
            for s in range(SLOTS):
                slot(PAIRS - 1, 1, s)
            for s in range(last_slot + 1):
                slot(PAIRS, 0, s)

        @block.sync
        def _(sp):
            wo_v = w_out.rearrange("(b p) n -> b p n", p=P)

            def load_w(n, half, buf, columns):
                wait(sp, w_ready, n - 1)
                sp.dma_start(w_raw[:, buf, :], w_in[bass.ds(columns, 1), half, :, :]
                             .rearrange("a p n -> (a p) n")).then_inc(w_loaded[buf], 16)

            def swap_k(p, par):
                sp.wait_ge(qk_split, 4 * p + 2)
                wait(sp, z_ready, SLOTS * p - SLOTS)
                for hh in range(2):
                    for to in range(2):
                        sp.dma_start(k_of(par, hh, True)[HD * to:HD * to + HD, :].bitcast(F32),
                                     k_of(par, hh, False)[HD * (1 - to):HD * (1 - to) + HD, :].bitcast(F32)
                                     ).then_inc(k_swapped, 16)

            for b in (1, 3):
                load_x_block(sp, b)
            kinds = (1, 2, 0)
            for n in range(2 * UNITS0):
                load_w(n, n % 2, n % 2, kinds[n // 2] * KB)
                if n == 1:
                    for b in (5, 7):
                        load_x_block(sp, b)
            for half in range(2):
                load_w(2 * UNITS0 + half, half, half, KB + 1)
            swap_k(0, 0)

            def slot(p, par, s):
                if s % 4 < 2 and not (isinstance(p, int) and p >= PAIRS - 1):
                    m = s // 4
                    columns = p + (2 * KB + 1, 1, 3 * KB, KB + 2)[m]
                    load_w(2 * (UNITS0 + 1 + m) + 8 * p + s % 4, s % 4, s % 4, columns)
                if s in (3, 7) and not is_first(p) and not is_tail(p):
                    half = s // 4
                    sp.wait_ge(o_lo, 2 * p - 1 + half)
                    for dram, hl in ((o_hi_dram, 0), (o_lo_dram, 1)):
                        sp.dma_start(dram[bass.ds(p - 1, 1), :, half * HALF:(half + 1) * HALF]
                                     .rearrange("a p n -> (a p) n"),
                                     o_split[:, hl, :].bitcast(F32)).then_inc(o_stored, 16)
                if s == 5 and not (isinstance(p, int) and p >= PAIRS - 1):
                    swap_k(p + 1, 1 - par)

            for s in range(SLOTS):
                slot(0, 0, s)
            with sp.Fori(0, (PAIRS - 4) // 2) as two:
                for odd in range(2):
                    for s in range(SLOTS):
                        slot(two * 2 + (1 + odd), 1 - odd, s)
            for p in (PAIRS - 3, PAIRS - 2):
                for s in range(SLOTS):
                    if p == PAIRS - 2 and s in (12, 13):
                        n = 2 * UNITS0 + 8 * (PAIRS - 1) + s % 4
                        load_w(n, s % 4, s % 4, 3 * KB + PAIRS - 1)
                    else:
                        slot(p, p % 2, s)
            slot(PAIRS - 1, 1, 3)

            def load_wo(n):
                wait(sp, w_ready, 2 * UNITS0 + 8 * (PAIRS - 1) + 2)
                wait(sp, wo_ready, n - 1)
                sp.dma_start(w_raw[:, n % 2, :], wo_v[n % KB, :, (n // KB) * HALF:(n // KB + 1) * HALF]
                             ).then_inc(wo_loaded[n % 2], 16)

            def load_o(b):
                for dram, hl in ((o_hi_dram, 0), (o_lo_dram, 1)):
                    sp.dma_start(hT[:, hl, b, :].bitcast(F32), dram[b]).then_inc(o_loaded[b], 16)

            load_wo(0)
            load_wo(1)
            sp.wait_ge(proj_done, 2 * UNITS0 + 8 * (PAIRS - 1) + 2)
            sp.wait_ge(o_stored, 64 * (PAIRS - 2))
            for b in range(PAIRS - 2):
                load_o(b)
            load_wo(2)
            load_wo(3)
            slot(PAIRS - 1, 1, 7)
            load_wo(4)
            load_wo(5)
            sp.wait_ge(o_stored, 64 * (PAIRS - 1))
            load_o(PAIRS - 2)
            load_wo(6)
            load_wo(7)

            def load_x(n):
                wait(sp, y_sum, n - 3)
                if n == 0:
                    sp.wait_ge(t_done, t_base(PAIRS))
                b, nh = n % KB, n // KB
                sp.dma_start(a_g[0][:, n % 4, :], x[b * P:(b + 1) * P, nh * HALF:(nh + 1) * HALF]
                             ).then_inc(xr_loaded[n % 4], 16)

            sp.wait_ge(a_ready, SLOTS * PAIRS)
            sp.dma_start(rest[:, 1, 0:S], final_g.rearrange("(a n) -> a n", a=1).to_broadcast([P, S])
                         ).then_inc(fg_loaded, 16)
            for n in range(4):
                load_x(n)
            load_wo(KB)
            load_wo(KB + 1)
            for n in range(4, 2 * KB):
                if n + 6 < 2 * KB:
                    load_wo(n + 6)
                load_x(n)

        @block.tensor
        def _(pe):
            def project(ring, bank, half, b):
                for n, (wl, hl) in enumerate(((0, 0), (0, 1), (1, 0))):
                    mm = nc.tensor.matmul(bank[:, :], w_split[:, ring, wl, b, :],
                                          hT[:, hl, b, half * HALF:(half + 1) * HALF],
                                          start=(b == 0 and n == 0), stop=(b == KB - 1 and n == 2))
                return mm

            def transpose_v(t_index, t_bank, half_index, buf):
                pe.wait_ge(stage_ready, half_index + 1)
                wait(pe, t_lo, t_index - 1)
                for b in range(GQ):
                    last = nc.tensor.transpose(t_ps[t_bank][:, b * P:(b + 1) * P],
                                               stage[:, buf, b * P:(b + 1) * P], ident[:, :])
                last.then_inc(t_done, 1)

            def transpose_x(n):
                half, b = n // KB, n % KB
                wait(pe, xt_lo, n - 3)
                for i in range(4):
                    pe.wait_ge(x_scaled, 4 * half + i + 1)
                    last = nc.tensor.transpose(four_banks[n % 4][:, i * P:(i + 1) * P],
                                               x_blocks[4 * half + i][:, b * P:(b + 1) * P], ident[:, :])
                last.then_inc(xt_done, 1)

            pe.wait_ge(consts_ready, 3)
            for n in range(4):
                transpose_x(n)
            for h, (kind, half) in enumerate(PROLOGUE):
                unit = "kvq".index(kind)
                wait(pe, stage_ready, h - 1)
                for b in range(KB):
                    pe.wait_ge(xt_lo, KB * half + b + 1)
                    pe.wait_ge(w_ready, 2 * unit + b // 4 + 1)
                    mm = project(unit % 2, (proj_ps, o_ps)[h % 2], half, b)
                    if h < 2 and KB * h + b + 4 < 2 * KB:
                        transpose_x(KB * h + b + 4)
                mm.then_inc(proj_done, 1)
                if h in (2, 4):
                    transpose_v(h // 2 - 1, h // 2 - 1, h - 1, 1)

            early = list(EARLY)

            def project_out(n, b):
                nh, tokens = n // KB, slice((n % KB) * P, (n % KB + 1) * P)
                if n % KB == 0:
                    pe.wait_ge(wo_ready, n + b + 1)
                if n == 0 and b < PAIRS - 1:
                    pe.wait_ge(o_loaded[b], 32)
                if n == 0 and b == PAIRS - 1:
                    pe.wait_ge(o_lo, 2 * PAIRS)
                if b == 0:
                    if n == 0:
                        pe.wait_ge(stage_ready, 2 * UNITS0 + 8 * (PAIRS - 1) + 2)
                    elif n < EARLY_TILES:
                        pe.wait_ge(beta_ready, SLOTS * PAIRS)
                    wait(pe, y_sum, n - EARLY_TILES + 1)
                for m, (ol, wl) in enumerate(((0, 0), (0, 1), (1, 0))):
                    mm = nc.tensor.matmul(y_banks[n % EARLY_TILES][:, :], hT[:, ol, b, tokens],
                                          w_out_of(nh, wl)[:, b, :],
                                          start=(b == 0 and m == 0), stop=(b == KB - 1 and m == 2))
                return mm

            def slot(p, par, s):
                hh, i = s // 8, s % 8
                width = P * (i + 1)
                if not is_tail(p):
                    if s == 0:
                        pe.wait_ge(qk_split, 4 * p + 4)
                        pe.wait_ge(k_swapped, 64 * p + 64)
                        if is_first(p):
                            pe.wait_ge(xt_lo, 2 * KB)
                    wait(pe, beta_ready, SLOTS * p + s - 1)
                    z = z_ps[s % 2]
                    q = q_of(par, hh)[:, i * P:(i + 1) * P]
                    for c in range(0, width, HALF):
                        n = max(min(width - c, HALF), 2 * P)
                        diagonal = c + HALF >= width
                        for swapped in (False, True):
                            mm = nc.tensor.matmul(z[:, c:c + n], q, k_of(par, hh, swapped)[:, c:c + n],
                                                  start=not swapped, stop=swapped and not diagonal)
                    mm = nc.tensor.matmul(z[:, i * P:(i + 1) * P], ident_bf[:, :], mask_bf[:, :],
                                          start=False, stop=True)
                    mm.then_inc(z_ready, 1)
                    if v_t_at(p, s) is not None:
                        t = v_t_at(p, s)
                        transpose_v(t_base(p) + t, t % 2, 2 * UNITS0 + 8 * p + 2 + (s == 8), int(s == 8))
                if not is_tail(p) and s in proj_slots(p):
                    half, part = (s % 4) // 2, s % 2
                    if half == 0:
                        pe.wait_ge(w_ready, 2 * UNITS0 + 8 * p + 2 * (s // 4) + part + 1)
                    if part == 0:
                        pe.wait_ge(stage_ready, 2 * UNITS0 + 8 * p + s // 2)
                    for b in range(4 * part, 4 * part + 4):
                        mm = project((UNITS0 + s // 4) % 2, proj_ps, half, b)
                    if part == 1:
                        mm.then_inc(proj_done, 1)
                if isinstance(p, int):
                    for _ in range(EARLY_BY_SLOT.get((p, s), 0)):
                        project_out(*early.pop(0))
                for t, av, ahh, grp, j in av_at(p, s):
                    apar = 1 - par if s < 5 else par
                    pe.wait_ge(t_lo, t_base(p) + t + 1)
                    if j == 0:
                        group = {1: -1, 5: 0, 9: 1, 13: 2}[s]
                        wait(pe, o_summed, 4 * p + group)
                    rel = max(0, j - GQ * grp)
                    for hl in range(2):
                        if rel == GQ - 1:
                            c, moving = HALF - 2 * P, aT_pad[:, hl, :]
                        else:
                            c = rel * P
                            moving = aT[:, av % 2, hl, c:HALF]
                        mm = nc.tensor.matmul(o_ps[:, c:HALF], v_of(apar)[:, j, 2 * ahh:2 * ahh + 2, :]
                                              .rearrange("p x d -> p (x d)"), moving,
                                              start=(j == 0 and hl == 0),
                                              stop=(j == GQ * (grp + 1) - 1 and hl == 1))
                    mm.then_inc(av_done, 1)
                for t, av, thh, grp, j in units_at(p, s):
                    wait(pe, t_lo, t_base(p) + t - 1)
                    if j == 0:
                        pe.wait_ge(a_ready, SLOTS * p + (0 if s < 4 else 4 * (s // 4)))
                    for i2 in range(max(0, j - GQ * grp), GQ):
                        last = nc.tensor.transpose(t_ps[t % 2][:, i2 * P:(i2 + 1) * P],
                                                   a_g[grp][:, i2, j * P:(j + 1) * P], ident[:, :])
                    last.then_inc(t_done, 1)

            over_pairs(pe, slot, 4)

            while early:
                project_out(*early.pop(0))
            for n in range(2 * KB):
                for b in range(PAIRS - 1 if n < EARLY_TILES else 0, KB):
                    mm = project_out(n, b)
                mm.then_inc(y_done, 1)

        @block.scalar
        def _(act):
            for b in range(0, KB, 2):
                load_x_block(act, b)
            act.wait_ge(consts_ready, 3)

            def root(cols, ready, count):
                act.wait_ge(ready, count)
                nc.scalar.activation(rstd[:, cols], ssq[:, cols], ACT.Sqrt, scale=1.0 / D,
                                     bias=eps_col[:, :]).then_inc(root_ready, 1)

            nc.scalar.activation(newton[:, 0:1], eps_col[:, :], ACT.Sqrt).then_inc(table_loaded, 1)

            def square_x(n, b):
                act.wait_ge(x_loaded[b], 16)
                wait(act, x_squared, n)
                nc.scalar.activation(oT[:, :], x_blocks[b], ACT.Square,
                                     accum_out=ssq[:, b:b + 1]).then_inc(x_squared, 1)

            def hi_x(n):
                half, b = n // KB, n % KB
                act.wait_ge(xt_done, n + 1)
                nc.scalar.activation(hT[:, 0, b, half * HALF:(half + 1) * HALF], four_banks[n % 4][:, :],
                                     ACT.Copy, scale=g_col[:, b:b + 1]).then_inc(xt_hi, 1)

            square_x(0, 0)
            square_x(1, 2)
            act.wait_ge(x_squared_dve, 2)
            root(slice(0, 4), x_squared, 2)
            for n, b in enumerate((4, 5, 6, 7)):
                square_x(2 + n, b)
            root(slice(4, 8), x_squared, 6)
            act.wait_ge(g_loaded, 16)

            def v_hi(par, half, t_index, t_bank):
                act.wait_ge(t_done, t_index + 1)
                nc.scalar.activation(v_of(par)[:, GQ * half:GQ * half + GQ, 0:4:3, :],
                                     t_ps[t_bank][:, :].rearrange("p (b x d) -> p b x d", b=GQ, x=2),
                                     ACT.Copy).then_inc(t_hi, 1)

            def to_stage(bank, h, buf):
                act.wait_ge(proj_done, h + 1)
                nc.scalar.activation(stage[:, buf, :], bank[:, :], ACT.Copy).then_inc(stage_ready, 1)

            for n in range(KB):
                hi_x(n)
            for h, (kind, half) in enumerate(PROLOGUE):
                if h in (2, 4):
                    act.wait_ge(qk_split, h // 2)
                if h in (3, 5):
                    act.wait_ge(t_done, h // 2)
                to_stage((proj_ps, o_ps)[h % 2], h, h % 2)
                if h == 0:
                    for n in range(KB, 2 * KB):
                        hi_x(n)
                if h in (3, 5):
                    v_hi(0, h // 2 - 1, h // 2 - 1, h // 2 - 1)

            def slot(p, par, s):
                evac = evac_at(p, s)
                if evac:
                    kind, half, h = evac
                    if kind == "g" and not is_last(p) or kind == "g" and s == 0:
                        act.wait_ge(qk_split, 4 * p + (4 if s == 0 else 7 + half))
                    elif kind == "v":
                        act.wait_ge(qk_split, 4 * p + 5 + half)
                    elif kind == "q":
                        act.wait_ge(t_done, t_base(p) + STEADY[8 if half else 6][0] + 1)
                    elif is_first(p):
                        act.wait_ge(qk_split, 3 + half)
                    else:
                        act.wait_ge(gate_ready, 2 * p - 1 + half)
                    to_stage(proj_ps, h, half)
                if gate_at(p, s):
                    half, number = gate_at(p, s)
                    act.wait_ge(stage_ready, 2 * UNITS0 + 8 * (PAIRS - 1) + 2 if is_last(p) and s == 6 else evac[2] + 1)
                    wait(act, o_gated, number - 1)
                    nc.scalar.activation(gate[:, half * HALF:(half + 1) * HALF], stage[:, half, :],
                                         ACT.Sigmoid).then_inc(gate_sig, 1)
                if s % 4 == 1 and av_at(p, s - 1) and (not is_tail(p) or s < 9):
                    _, av, ohh, grp, _ = av_at(p, s - 1)[-1]
                    act.wait_ge(av_done, av_base(p) + av + 1)
                    if ohh == 0:
                        wait(act, o_lo, 2 * p - 1 + grp)
                    rows = slice(HD * ohh, HD * ohh + HD)
                    other = slice(HD - HD * ohh, 2 * HD - HD * ohh)
                    nc.scalar.activation(oT[rows, grp * HALF:(grp + 1) * HALF], o_ps[other, :],
                                         ACT.Copy).then_inc(o_shift, 1)
                for t, av, _, grp, j in (units_at(p, s - 1) if s else av_at(p, 0)):
                    rel = max(0, j - GQ * grp)
                    act.wait_ge(t_done, t_base(p) + t + 1)
                    wait(act, av_done, av_base(p) + av - 1)
                    to = aT_pad[:, 0, P:2 * P] if rel == GQ - 1 else aT[:, av % 2, 0, rel * P:HALF]
                    nc.scalar.activation(to, t_ps[t % 2][:, rel * P:HALF], ACT.Copy).then_inc(t_hi, 1)
                if s in (2, 6) and not is_first(p):
                    half = s // 4
                    act.wait_ge(o_gated, 2 * p - 1 + half)
                    if not is_tail(p):
                        wait(act, o_stored, 64 * (p - 1) + 32 * half)
                    nc.scalar.activation(split_of(p, half)[0], oT[:, half * HALF:(half + 1) * HALF],
                                         ACT.Copy).then_inc(o_hi, 1)
                if is_tail(p):
                    return
                hh, i = s // 8, s % 8
                width, grp = P * (i + 1), i // GQ
                act.wait_ge(z_ready, SLOTS * p + s + 1)
                wait(act, a_ready, SLOTS * p + s - 1)
                nc.scalar.activation(rest[:, s % 2, S - width:S], z_ps[s % 2][:, 0:width], ACT.Sigmoid,
                                     scale=-SCALE).then_inc(rest_ready, 1)
                nc.scalar.activation(a_g[grp][:, i % GQ, 0:width], z_ps[s % 2][:, 0:width], ACT.Sigmoid,
                                     scale=SCALE).then_inc(beta_ready, 1)
                if v_t_at(p, s) is not None:
                    t = v_t_at(p, s)
                    v_hi(1 - par, s // 8, t_base(p) + t, t % 2)

            over_pairs(act, slot)

            for n in range(2 * KB):
                act.wait_ge(y_sum, n + 1)
                wait(act, y_squared, n)
                nc.scalar.activation(rest[:, 0, 0:HALF], y_of(n), ACT.Square, accum_out=ssq[:, n:n + 1]
                                     ).then_inc(y_squared, 1)
                if n >= KB:
                    b = n - KB
                    root(slice(b, b + 1), ssq_summed, b + 1)
                    for half in range(2):
                        act.wait_ge(out_ready, 2 * b + half + 1)
                        cols = slice(half * HALF, (half + 1) * HALF)
                        act.dma_start(out[b * P:(b + 1) * P, cols], out_of(b)[half]).then_inc(stored[b % 2], 16)
            for odd in range(2):
                act.wait_ge(stored[odd], 16 * KB)

        @block.vector
        def _(dve):
            def split_hi_w(ring, part):
                nc.vector.tensor_copy(w_split[:, ring, 0, 4 * part:4 * part + 4, :],
                                      w_raw[:, part, :].rearrange("p (b n) -> p b n", b=4)).then_inc(w_hi, 1)

            def rsqrt(cols, n):
                r, m, t = rstd[:, cols], mean_sq[:, cols], newton[:, cols]
                nc.vector.tensor_scalar(m, ssq[:, cols], 1.0 / D, EPS, ALU.mult, ALU.add).then_inc(mean_ready, 1)
                dve.wait_ge(root_ready, n + 1)
                nc.vector.reciprocal(r, r).then_inc(rstd_ready, 1)
                dve.wait_ge(mean_ready, n + 1)
                dve.wait_ge(rstd_ready, 5 * n + 1)
                nc.vector.tensor_tensor(t, r, r, ALU.mult).then_inc(rstd_ready, 1)
                dve.wait_ge(rstd_ready, 5 * n + 2)
                nc.vector.tensor_tensor(t, t, m, ALU.mult).then_inc(rstd_ready, 1)
                dve.wait_ge(rstd_ready, 5 * n + 3)
                nc.vector.tensor_scalar(t, t, -0.5, 1.5, ALU.mult, ALU.add).then_inc(rstd_ready, 1)
                dve.wait_ge(rstd_ready, 5 * n + 4)
                nc.vector.tensor_tensor(r, r, t, ALU.mult).then_inc(rstd_ready, 1)
                dve.wait_ge(rstd_ready, 5 * n + 5)

            nc.vector.memset(aT_pad[:, :, 0:P].bitcast(F32), 0.0)
            nc.vector.memset(eps_col[:, :], EPS)
            nc.vector.memset(rest[:, :, S:S + 1], 1.0).then_inc(consts_ready, 1)
            def square_x(n, b):
                dve.wait_ge(x_loaded[b], 16)
                wait(dve, x_squared_dve, n)
                nc.vector.tensor_tensor_reduce(gate[:, :], x_blocks[b], x_blocks[b], 1.0, 0.0, ALU.mult, ALU.add,
                                               ssq[:, b:b + 1]).then_inc(x_squared_dve, 1)

            def scale_x(half):
                rsqrt(slice(4 * half, 4 * half + 4), half)
                for b in range(4 * half, 4 * half + 4):
                    nc.vector.tensor_scalar(x_blocks[b], x_blocks[b], rstd[:, b:b + 1], None,
                                            ALU.mult).then_inc(x_scaled, 1)

            def lo_x(n):
                half, b = n // KB, n % KB
                cols = slice(half * HALF, (half + 1) * HALF)
                dve.wait_ge(xt_hi, n + 1)
                nc.vector.scalar_tensor_tensor(hT[:, 1, b, cols], four_banks[n % 4][:, :], g_col[:, b:b + 1],
                                               hT[:, 0, b, cols].bitcast(F32), ALU.mult, ALU.subtract
                                               ).then_inc(xt_lo, 1)

            def next_w(n):
                dve.wait_ge(w_loaded[n % 2], 16 * (n // 2 + 1))
                split_hi_w((n // 2) % 2, n % 2)

            square_x(0, 1)
            square_x(1, 3)
            dve.wait_ge(table_loaded, 1)
            dve.wait_ge(x_squared_dve, 2)
            dve.wait_ge(x_squared, 2)
            scale_x(0)
            next_w(0)
            next_w(1)
            dve.wait_ge(g_loaded, 16)
            for n in range(KB):
                lo_x(n)
                if n in (1, 3):
                    next_w(2 + n // 2)
            dve.wait_ge(x_squared, 6)
            scale_x(1)

            def split_heads(kind, par, half, h, buf, count):
                dve.wait_ge(stage_ready, h + 1)
                cols = slice(half * HALF, (half + 1) * HALF)
                for hh in range(2):
                    rows = slice(HD * hh, HD * hh + HD)
                    to = q_of(par, hh) if kind == "q" else k_of(par, hh, False)
                    last = nc.vector.tensor_copy(to[rows, cols], stage[rows, buf, :])
                last.then_inc(qk_hi, 1)
                dve.wait_ge(qk_hi, count)
                for hh in range(2):
                    rows = slice(HD * hh, HD * hh + HD)
                    other = slice(HD - HD * hh, 2 * HD - HD * hh)
                    to = q_of(par, hh) if kind == "q" else k_of(par, hh, False)
                    last = nc.vector.tensor_tensor(to[other, cols], stage[rows, buf, :],
                                                   to[rows, cols].bitcast(F32), ALU.subtract)
                last.then_inc(qk_split, 1)

            def v_lo(par, half, t_index, t_bank):
                dve.wait_ge(t_hi, t_index + 1)
                blocks = slice(GQ * half, GQ * half + GQ)
                nc.vector.tensor_tensor(v_of(par)[:, blocks, 1:3, :],
                                        t_ps[t_bank][:, :].rearrange("p (b x d) -> p b x d", b=GQ, x=2),
                                        v_of(par)[:, blocks, 0:4:3, :].bitcast(F32), ALU.subtract
                                        ).then_inc(t_lo, 1)

            for n in range(KB, 2 * KB):
                lo_x(n)
                if n == KB + 2:
                    split_heads("k", 0, 0, 0, 0, 1)
            for h, (kind, half) in enumerate(PROLOGUE):
                if h in (2, 4, 5):
                    split_heads(kind, 0, half, h, h % 2, {2: 2, 4: 3, 5: 4}[h])
                if h in (3, 5):
                    v_lo(0, h // 2 - 1, h // 2 - 1, h // 2 - 1)
                if h in (2, 3):
                    dve.wait_ge(proj_done, h + 1)
                    next_w(2 * h)
                    next_w(2 * h + 1)

            def wo_hi_part(n):
                dve.wait_ge(wo_loaded[n % 2], 16 * (n // 2 + 1))
                dve.wait_ge(av_done, AV_PER_PAIR * (PAIRS - 1 + n // KB))
                nc.vector.tensor_copy(w_out_of(n // KB, 0)[:, n % KB, :], w_raw[:, n % 2, :]).then_inc(wo_hi, 1)

            def slot(p, par, s):
                evac = evac_at(p, s)
                if evac:
                    kind, half, h = evac
                    if kind in "kq":
                        split_heads(kind, 1 - par, half, h, half,
                                    4 * p + 5 + half + (2 if kind == "q" else 0))
                if gate_at(p, s):
                    half, number = gate_at(p, s)
                    dve.wait_ge(gate_sig, number + 1)
                    cols = slice(half * HALF, (half + 1) * HALF)
                    nc.vector.tensor_tensor(gate[:, cols], stage[:, half, :], gate[:, cols], ALU.mult
                                            ).then_inc(gate_ready, 1)
                if s % 4 == 1 and av_at(p, s - 1) and (not is_tail(p) or s < 9):
                    _, _, ohh, grp, _ = av_at(p, s - 1)[-1]
                    group = {1: -1, 5: 0, 9: 1, 13: 2}[s]
                    dve.wait_ge(o_shift, 4 * p + group)
                    rows = slice(HD * ohh, HD * ohh + HD)
                    cols = slice(grp * HALF, (grp + 1) * HALF)
                    nc.vector.tensor_tensor(oT[rows, cols], o_ps[rows, :], oT[rows, cols], ALU.add
                                            ).then_inc(o_summed, 1)
                for t, av, _, grp, j in (units_at(p, s - 1) if s else av_at(p, 0)):
                    rel = max(0, j - GQ * grp)
                    dve.wait_ge(t_hi, t_base(p) + t + 1)
                    if rel == GQ - 1:
                        hi, lo = aT_pad[:, 0, P:2 * P], aT_pad[:, 1, P:2 * P]
                    else:
                        hi, lo = aT[:, av % 2, 0, rel * P:HALF], aT[:, av % 2, 1, rel * P:HALF]
                    nc.vector.tensor_tensor(lo, t_ps[t % 2][:, rel * P:HALF], hi.bitcast(F32), ALU.subtract
                                            ).then_inc(t_lo, 1)
                if s in (2, 6) and not is_first(p):
                    half = s // 4
                    dve.wait_ge(o_hi, 2 * p - 1 + half)
                    hi, lo = split_of(p, half)
                    nc.vector.tensor_tensor(lo, oT[:, half * HALF:(half + 1) * HALF], hi.bitcast(F32),
                                            ALU.subtract).then_inc(o_lo, 1)
                if is_tail(p):
                    return
                width = P * (s % 8 + 1)
                span = rest[:, s % 2, S - 1:(S - 1 - width if width < S else None):-1]
                dve.wait_ge(rest_ready, SLOTS * p + s + 1)
                nc.vector.tensor_tensor_scan(span, span, span, 1.0, ALU.mult, ALU.bypass
                                             ).then_inc(scan_done, 1)
                if v_t_at(p, s) is not None:
                    t = v_t_at(p, s)
                    v_lo(1 - par, s // 8, t_base(p) + t, t % 2)
                if s % 4 in (1, 2) and not is_last(p):
                    part = s % 4 - 1
                    unit = UNITS0 + 4 * p + s // 4 + 1
                    dve.wait_ge(proj_done, 2 * unit - 2)
                    dve.wait_ge(w_loaded[part], 16 * unit + 16)
                    split_hi_w((UNITS0 + 1 + s // 4) % 2, part)
                if is_last(p) and 5 <= s < 5 + KB:
                    wo_hi_part(s - 5)

            over_pairs(dve, slot)

            for n in range(2 * KB):
                b = n % KB
                if n < KB:
                    wo_hi_part(KB + n)
                dve.wait_ge(y_done, n + 1)
                dve.wait_ge(xr_loaded[n % 4], 16 * (n // 4 + 1))
                wait(dve, y_squared, n - 1)
                if n >= KB + 2:
                    dve.wait_ge(out_ready, 2 * (n - KB) - 2)
                nc.vector.tensor_tensor(y_of(n), y_banks[n % EARLY_TILES][:, :], a_g[0][:, n % 4, :], ALU.add
                                        ).then_inc(y_sum, 1)
                if n < KB:
                    continue
                dve.wait_ge(y_squared, n + 1)
                r = rstd[:, b:b + 1]
                nc.vector.tensor_tensor(ssq[:, b:b + 1], ssq[:, b:b + 1], ssq[:, n:n + 1], ALU.add
                                        ).then_inc(ssq_summed, 1)
                dve.wait_ge(ssq_summed, b + 1)
                rsqrt(slice(b, b + 1), 2 + b)
                if b == 0:
                    dve.wait_ge(fg_loaded, 16)
                wait(dve, stored[b % 2], 32 * (b // 2))
                for half in range(2):
                    nc.vector.scalar_tensor_tensor(out_of(b)[half], y_of(b + KB * half), r,
                                                   rest[:, 1, half * HALF:(half + 1) * HALF],
                                                   ALU.mult, ALU.mult).then_inc(out_ready, 1)

        @block.gpsimd
        def _(pool):
            pool.dma_start(g_col[:, :], norm_g).then_inc(g_loaded, 16)
            nc.gpsimd.memset(ident[:, :], 0.0)
            nc.gpsimd.memset(mask_bf[:, :], 0.0)
            nc.gpsimd.memset(ident_bf[:, :], 0.0).then_inc(zeros_ready, 1)
            pool.wait_ge(zeros_ready, 1)
            for t in (ident, ident_bf):
                last = nc.gpsimd.affine_select(out=t[:, :], in_=t[:, :], compare_op=ALU.not_equal, fill=1.0,
                                               base=0, pattern=[[-1, P]], channel_multiplier=1)
            nc.gpsimd.affine_select(out=mask_bf[:, :], in_=mask_bf[:, :], compare_op=ALU.is_gt, fill=MASKED,
                                    base=0, pattern=[[-1, P]], channel_multiplier=1).then_inc(consts_ready, 2)

            def lo_w(n, ring, part):
                pool.wait_ge(w_hi, n + 1)
                to = w_split[:, ring, :, 4 * part:4 * part + 4, :]
                nc.gpsimd.tensor_tensor(to[:, 1], w_raw[:, part, :].rearrange("p (b n) -> p b n", b=4),
                                        to[:, 0].bitcast(F32), ALU.subtract).then_inc(w_ready, 1)

            def lo_wo(n):
                pool.wait_ge(wo_hi, n + 1)
                nc.gpsimd.tensor_tensor(w_out_of(n // KB, 1)[:, n % KB, :], w_raw[:, n % 2, :],
                                        w_out_of(n // KB, 0)[:, n % KB, :].bitcast(F32), ALU.subtract
                                        ).then_inc(wo_ready, 1)

            for n in range(2 * UNITS0 + 2):
                lo_w(n, (n // 2) % 2, n % 2)

            def slot(p, par, s):
                if s in (1, 5) and not is_first(p):
                    half = s // 4
                    pool.wait_ge(o_summed, 4 * p - 1 + half)
                    pool.wait_ge(gate_ready, 2 * p - 1 + half)
                    cols = slice(half * HALF, (half + 1) * HALF)
                    nc.gpsimd.tensor_tensor(oT[:, cols], oT[:, cols], gate[:, cols], ALU.mult
                                            ).then_inc(o_gated, 1)
                if is_tail(p):
                    return
                i = s % 8
                width = P * (i + 1)
                a = a_g[i // GQ][:, i % GQ, 0:width]
                pool.wait_ge(beta_ready, SLOTS * p + s + 1)
                pool.wait_ge(scan_done, SLOTS * p + s + 1)
                nc.gpsimd.tensor_tensor(a, a, rest[:, s % 2, S + 1 - width:S + 1], ALU.mult
                                        ).then_inc(a_ready, 1)
                if s % 4 in (1, 2) and not is_last(p):
                    n = 2 * (UNITS0 + 4 * p + s // 4 + 1) + s % 4 - 1
                    lo_w(n, (UNITS0 + 1 + s // 4) % 2, s % 4 - 1)
                if is_last(p) and 5 <= s < 5 + KB:
                    lo_wo(s - 5)

            over_pairs(pool, slot)

            for n in range(KB, 2 * KB):
                lo_wo(n)


def kernel(**inputs):
    import numpy as _np
    import concourse.bacc as _bacc
    from concourse.bass_utils import run_bass_kernel_spmd as _run

    nc = _bacc.Bacc("TRN2", target_bir_lowering=False, num_devices=1)
    arrays = {
        "x": inputs["x"].reshape(S, D),
        "norm_g": inputs["norm_g"].reshape(KB, P).T,
        "w_in": inputs["sb_w_in"].reshape(2, GQ, P, 4 * KB, P).transpose(3, 0, 2, 1, 4)
                                 .reshape(4 * KB, 2, P, HALF),
        "w_out": inputs["sb_w_out"].reshape(D, D),
        "final_g": inputs["final_g"].reshape(D),
    }
    arrays = {name: _np.ascontiguousarray(a) for name, a in arrays.items()}
    aps = {name: nc.dram_tensor(name, a.shape, F32, kind="ExternalInput").ap() for name, a in arrays.items()}
    out = nc.dram_tensor("out", [S, D], F32, kind="ExternalOutput").ap()
    stick_breaking_layer(nc, aps["x"], aps["norm_g"], aps["w_in"], aps["w_out"], aps["final_g"], out)
    r = _run(nc, [arrays], core_ids=[0])
    return r.results[0]["out"].reshape(1, S, D)
```

```python
from contextlib import ExitStack

import concourse.bass as bass
from concourse import mybir

ALU = mybir.AluOpType
ACT = mybir.ActivationFunctionType
F32 = mybir.dt.float32
F32R = mybir.dt.float32r
BF16 = mybir.dt.bfloat16

P = 128
D = 1024
S = 1024
HEADS = 16
HD = D // HEADS
PAIRS = HEADS // 2
KB = D // P
HALF = 512
GQ = HALF // P
SLOTS = 16
EPS = 1e-6
MASKED = -1e30
SCALE = HD ** -0.5

UNITS0 = 3
T_PER_PAIR, AV_PER_PAIR = 26, 24


def plan(with_v):
    out, t, av = [], 0, 0
    for s in range(SLOTS):
        v_t = None
        if with_v and s in (6, 8):
            v_t, t = t, t + 1
        hh, grp = ((1, 1), (0, 0), (0, 1), (1, 0))[s // 4]
        blocks = (2 * (s % 4), 2 * (s % 4) + 1) if grp else (s % 4,)
        units = []
        for j in blocks:
            units.append((t, av, hh, grp, j))
            t, av = t + 1, av + 1
        out.append((v_t, units))
    return out


STEADY, LAST = plan(True), plan(False)
FIRST_SKIPS = 8


def t_base(p):
    if isinstance(p, int) and p == PAIRS:
        return t_base(PAIRS - 1) + T_PER_PAIR - 2
    return T_PER_PAIR * p + (2 - FIRST_SKIPS)


def av_base(p):
    return AV_PER_PAIR * p - FIRST_SKIPS


def is_last(p):
    return isinstance(p, int) and p == PAIRS - 1


def is_tail(p):
    return isinstance(p, int) and p == PAIRS


def is_first(p):
    return isinstance(p, int) and p == 0


def wait(eng, sem, value):
    if not isinstance(value, int) or value > 0:
        eng.wait_ge(sem, value)


def units_at(p, s):
    if isinstance(p, int) and (p == 0 and s < 4 or p == PAIRS and s >= 4):
        return []
    return (LAST if isinstance(p, int) and p >= PAIRS - 1 else STEADY)[s][1]


def av_at(p, s):
    if s > 0:
        return units_at(p, s - 1)
    return [] if is_first(p) else [(-1, -1, 1, 0, GQ - 1)]


def v_t_at(p, s):
    return None if isinstance(p, int) and p >= PAIRS - 1 else STEADY[s][0]


def proj_slots(p):
    return range(SLOTS // 2) if is_last(p) else range(SLOTS)


def proj_part(p, s):
    if is_last(p):
        return s // 4, 2 * (s % 4), 2 * (s % 4) + 1
    return (s % 4) // 2, 4 * (s % 2), 4 * (s % 2) + 3


def kind_of(p, s):
    return "g" if is_last(p) else "kvqg"[s // 4]


def evac_at(p, s):
    if s % 2 or is_tail(p) or (is_first(p) and s == 0):
        return None
    number = 2 * UNITS0 + 8 * p + s // 2 - 1
    if s == 0:
        return "g", 1, number
    if is_last(p):
        return ("g", s // 4 - 1, 2 * UNITS0 + 8 * p + s // 4 - 1) if s in (4, 8) else None
    return kind_of(p, s - 1), ((s - 1) % 4) // 2, number


def gate_at(p, s):
    evac = evac_at(p, s)
    if not evac or evac[0] != "g":
        return None
    return evac[1], 2 * p - 1 if s == 0 else 2 * p + evac[1]


PROLOGUE = (("k", 0), ("v", 0), ("k", 1), ("v", 1), ("q", 0), ("q", 1))
BANKS = 5
PARTIAL_TILES = 2
ORDER = [*range(PARTIAL_TILES, KB), *range(PARTIAL_TILES), *range(KB, 2 * KB)]
EARLY = [(n, b) for n in [*range(PARTIAL_TILES), *ORDER[:BANKS]] for b in range(PAIRS - 1)]
EARLY_BY_SLOT = {(PAIRS - 1, s): n for s, n in zip(range(8, 16), (2, 2, 2, 1, 4, 3, 3, 3))}
EARLY_BY_SLOT |= {(PAIRS, s): 4 for s in range(5)}
X_COUNT = [sum(ORDER[m] >= PARTIAL_TILES for m in range(at % 4, at + 1, 4)) for at in range(2 * KB)]
PARTIAL_SLOTS = (11, 13)
WO_RING = 4
WO_BY_SLOT = {5: (0,), 6: (1,), 7: (2,), 8: (3, 4), 9: (5, 6), 10: (7,)}

WO_BY_TILE = {0: (0, 1), 1: (2,), 2: (3,), 3: (4,), 4: (5,), 5: (6, 7)}


def stick_breaking_layer(nc, x, norm_g, w_in, w_out, final_g, out):
    o_hi_dram = nc.dram_tensor("o_hi_scratch", [PAIRS, P, S], F32).ap()
    o_lo_dram = nc.dram_tensor("o_lo_scratch", [PAIRS, P, S], F32).ap()

    with ExitStack() as ctx:
        def sb(name, shape, dt=F32):
            return ctx.enter_context(nc.sbuf_tensor(name, shape, dt))

        def ps(name, shape, dt=F32):
            return ctx.enter_context(nc.psum_tensor(name, shape, dt))

        def sem(name):
            return ctx.enter_context(nc.semaphore(name))

        hT = sb("hT", [P, 2, KB, S], F32R)
        arena = sb("arena", [P, 2, 4, 2 * S], F32R)
        w_raw = sb("w_raw", [P, 2, HALF])
        a_g = [sb("a_group0", [P, GQ, HALF]), sb("a_group1", [P, GQ, S])]
        rest = sb("rest", [P, 2, S + 1])
        aT = sb("aT", [P, 2, 2, HALF], F32R)
        aT_pad = sb("aT_pad", [P, 2, 2 * P], F32R)
        stage = sb("stage", [P, 2, HALF])
        gate = sb("gate", [P, S])
        oT = sb("oT", [P, S])
        o_split = sb("o_split", [P, 2, HALF], F32R)
        ident = sb("ident", [P, P])
        ident_bf = sb("ident_bf", [P, P], BF16)
        mask_bf = sb("mask_bf", [P, P], BF16)
        g_col = sb("g_col", [P, KB])
        ssq = sb("ssq", [P, 2 * KB])
        rstd = sb("rstd", [P, KB])
        mean_sq = sb("mean_sq", [P, KB])
        newton = sb("newton", [P, KB])
        eps_col = sb("eps_col", [P, 1])
        with nc.sbuf_tensor("w_split", [P, 2, 2, KB, P], F32R) as w_split:
            pass
        wo_raw = sb("wo_raw", [P, WO_RING, HALF])

        x_blocks = ([a_g[1][:, b, :] for b in range(4)]
                    + [a_g[0][:, 2 * b:2 * b + 2, :].rearrange("p a n -> p (a n)") for b in range(2)]
                    + [rest[:, b, 0:S] for b in range(2)])

        def q_of(par, hh):
            return arena[:, par, 0, hh * S:(hh + 1) * S]

        def k_of(par, hh, swapped):
            return arena[:, par, 2 if swapped else 1, hh * S:(hh + 1) * S]

        def v_of(par):
            return arena[:, par, 3, :].rearrange("p (b x d) -> p b x d", b=KB, x=4)

        def w_out_of(half, hl):
            return arena[:, half, 2 * hl:2 * hl + 2, :].rearrange("p a (b n) -> p (a b) n", n=HALF)

        z_ps = [ps(f"z_ps{b}", [P, S]) for b in range(2)]
        t_ps = [ps(f"t_ps{b}", [P, HALF]) for b in range(2)]
        proj_ps = ps("proj_ps", [P, HALF])
        o_ps = ps("o_ps", [P, HALF])
        y_banks = [proj_ps] + [z[:, c:c + HALF] for z in z_ps for c in (0, HALF)]
        four_banks = y_banks[1:]

        x_loaded = [sem(f"x_loaded{b}") for b in range(KB)]
        g_loaded = sem("g_loaded")
        consts_ready = sem("consts_ready")
        x_squared = sem("x_squared")
        mean_ready = sem("mean_ready")
        root_ready = sem("root_ready")
        rstd_ready = sem("rstd_ready")
        x_scaled = sem("x_scaled")
        x_scaled_act = sem("x_scaled_act")
        xt_done = sem("xt_done")
        xt_hi = sem("xt_hi")
        xt_lo = sem("xt_lo")
        w_loaded = [sem(f"w_loaded{b}") for b in range(2)]
        w_hi = sem("w_hi")
        w_ready = sem("w_ready")
        proj_done = sem("proj_done")
        stage_ready = sem("stage_ready")
        qk_hi = sem("qk_hi")
        qk_split = sem("qk_split")
        gate_sig = sem("gate_sig")
        gate_ready = sem("gate_ready")
        k_swapped = sem("k_swapped")
        z_ready = sem("z_ready")
        rest_ready = sem("rest_ready")
        beta_ready = sem("beta_ready")
        scan_done = sem("scan_done")
        a_ready = sem("a_ready")
        t_done = sem("t_done")
        t_hi = sem("t_hi")
        t_lo = sem("t_lo")
        av_done = sem("av_done")
        o_shift = sem("o_shift")
        o_summed = sem("o_summed")
        o_gated = sem("o_gated")
        o_hi = sem("o_hi")
        o_lo = sem("o_lo")
        o_stored = sem("o_stored")
        o_loaded = [[sem(f"o_loaded{half}_{b}") for b in range(PAIRS - 1)] for half in range(2)]
        wo_loaded = [sem(f"wo_loaded{b}") for b in range(WO_RING)]
        wo_hi = sem("wo_hi")
        wo_ready = sem("wo_ready")
        xs_loaded = [sem(f"xs_loaded{n}") for n in range(PARTIAL_TILES)]
        partial_done = sem("partial_done")
        partial_sum = sem("partial_sum")
        y_done = sem("y_done")
        y_sum = sem("y_sum")
        y_squared = sem("y_squared")
        ssq_summed = sem("ssq_summed")
        y_weighted = sem("y_weighted")
        zeros_ready = sem("zeros_ready")
        xr_loaded = [sem(f"xr_loaded{b}") for b in range(4)]
        fg_loaded = sem("fg_loaded")
        out_ready = sem("out_ready")
        stored = [sem(f"stored{b}") for b in range(2)]
        table_loaded = sem("table_loaded")
        x_squared_dve = sem("x_squared_dve")

        block = ctx.enter_context(nc.Block())

        def wo_lo_part(engine, n):
            engine.tensor_tensor(w_out_of(n // KB, 1)[:, n % KB, :], wo_raw[:, n % WO_RING, :],
                                 w_out_of(n // KB, 0)[:, n % KB, :].bitcast(F32), ALU.subtract
                                 ).then_inc(wo_ready, 1)

        y_half = a_g[1][:, :, :].rearrange("p a (b n) -> p (a b) n", b=2)

        def y_of(n):
            return y_half[:, n, :] if n < KB else gate[:, (n % 2) * HALF:(n % 2 + 1) * HALF]

        def out_of(b):
            return [stage[:, 0, :], stage[:, 1, :]] if b % 2 else [oT[:, 0:HALF], oT[:, HALF:S]]

        def split_of(p, half):
            if is_tail(p):
                cols = slice(half * HALF, (half + 1) * HALF)
                return hT[:, 0, PAIRS - 1, cols], hT[:, 1, PAIRS - 1, cols]
            return o_split[:, 0, :], o_split[:, 1, :]

        def load_x_block(eng, b):
            eng.dma_start(x_blocks[b], x[b * P:(b + 1) * P, :]).then_inc(x_loaded[b], 16)

        def over_pairs(eng, slot, last_slot=6):
            for s in range(SLOTS):
                slot(0, 0, s)
            with eng.Fori(0, (PAIRS - 2) // 2) as two:
                for odd in range(2):
                    for s in range(SLOTS):
                        slot(two * 2 + (1 + odd), 1 - odd, s)
            for s in range(SLOTS):
                slot(PAIRS - 1, 1, s)
            for s in range(last_slot + 1):
                slot(PAIRS, 0, s)

        @block.sync
        def _(sp):
            wo_v = w_out.rearrange("(b p) n -> b p n", p=P)

            def load_w(n, half, buf, columns):
                wait(sp, w_ready, n - 1)
                sp.dma_start(w_raw[:, buf, :], w_in[bass.ds(columns, 1), half, :, :]
                             .rearrange("a p n -> (a p) n")).then_inc(w_loaded[buf], 16)

            def swap_k(p, par):
                sp.wait_ge(qk_split, 4 * p + 2)
                wait(sp, z_ready, SLOTS * p - SLOTS)
                for hh in range(2):
                    for to in range(2):
                        sp.dma_start(k_of(par, hh, True)[HD * to:HD * to + HD, :].bitcast(F32),
                                     k_of(par, hh, False)[HD * (1 - to):HD * (1 - to) + HD, :].bitcast(F32)
                                     ).then_inc(k_swapped, 16)

            for b in (1, 3):
                load_x_block(sp, b)
            kinds = (1, 2, 0)
            for n in range(2 * UNITS0):
                load_w(n, n % 2, n % 2, kinds[n // 2] * KB)
                if n == 1:
                    for b in (5, 7):
                        load_x_block(sp, b)
            for half in range(2):
                load_w(2 * UNITS0 + half, half, half, KB + 1)
            swap_k(0, 0)

            def slot(p, par, s):
                if s % 4 < 2 and not (isinstance(p, int) and p >= PAIRS - 1):
                    m = s // 4
                    columns = p + (2 * KB + 1, 1, 3 * KB, KB + 2)[m]
                    load_w(2 * (UNITS0 + 1 + m) + 8 * p + s % 4, s % 4, s % 4, columns)
                if s in (3, 7) and not is_first(p) and not is_tail(p):
                    half = s // 4
                    sp.wait_ge(o_lo, 2 * p - 1 + half)
                    for dram, hl in ((o_hi_dram, 0), (o_lo_dram, 1)):
                        sp.dma_start(dram[bass.ds(p - 1, 1), :, half * HALF:(half + 1) * HALF]
                                     .rearrange("a p n -> (a p) n"),
                                     o_split[:, hl, :].bitcast(F32)).then_inc(o_stored, 16)
                if s == 5 and not (isinstance(p, int) and p >= PAIRS - 1):
                    swap_k(p + 1, 1 - par)

            for s in range(SLOTS):
                slot(0, 0, s)
            with sp.Fori(0, (PAIRS - 4) // 2) as two:
                for odd in range(2):
                    for s in range(SLOTS):
                        slot(two * 2 + (1 + odd), 1 - odd, s)
            for p in (PAIRS - 3, PAIRS - 2):
                for s in range(SLOTS):
                    if p == PAIRS - 2 and s in (12, 13):
                        n = 2 * UNITS0 + 8 * (PAIRS - 1) + s % 4
                        load_w(n, s % 4, s % 4, 3 * KB + PAIRS - 1)
                    else:
                        slot(p, p % 2, s)

            def load_wo(n):
                if n == 0:
                    sp.wait_ge(proj_done, 2 * UNITS0 + 8 * (PAIRS - 1))
                wait(sp, wo_ready, n - WO_RING + 1)
                sp.dma_start(wo_raw[:, n % WO_RING, :], wo_v[n % KB, :, (n // KB) * HALF:(n // KB + 1) * HALF]
                             ).then_inc(wo_loaded[n % WO_RING], 16)

            def load_o(half, b):
                cols = slice(half * HALF, (half + 1) * HALF)
                for dram, hl in ((o_hi_dram, 0), (o_lo_dram, 1)):
                    sp.dma_start(hT[:, hl, b, cols].bitcast(F32), dram[b, :, cols]).then_inc(o_loaded[half][b], 16)

            for n in range(WO_RING):
                load_wo(n)
            slot(PAIRS - 1, 1, 3)
            sp.wait_ge(proj_done, 2 * UNITS0 + 8 * (PAIRS - 1) + 1)
            sp.wait_ge(o_stored, 64 * (PAIRS - 2))
            load_o(0, 0)
            load_o(0, 1)
            load_wo(4)
            load_o(0, 2)
            load_wo(5)
            load_o(0, 3)
            slot(PAIRS - 1, 1, 7)
            load_wo(6)
            load_o(0, 4)
            load_o(0, 5)
            load_wo(7)
            sp.wait_ge(o_stored, 64 * (PAIRS - 1))
            load_o(0, PAIRS - 2)
            for n in range(PARTIAL_TILES):
                sp.wait_ge(gate_ready, 2 * PAIRS - 1 + n)
                sp.dma_start(stage[:, n, :], x[n * P:(n + 1) * P, 0:HALF]).then_inc(xs_loaded[n], 16)
            sp.wait_ge(proj_done, 2 * UNITS0 + 8 * (PAIRS - 1) + 2)
            for b in range(PAIRS - 1):
                load_o(1, b)

            def load_x(n):
                wait(sp, y_sum, n - 3)
                if n == 0:
                    sp.wait_ge(t_done, t_base(PAIRS))
                if ORDER[n] < PARTIAL_TILES:
                    return
                b, nh = ORDER[n] % KB, ORDER[n] // KB
                sp.dma_start(a_g[0][:, n % 4, :], x[b * P:(b + 1) * P, nh * HALF:(nh + 1) * HALF]
                             ).then_inc(xr_loaded[n % 4], 16)

            for n in range(KB, KB + WO_RING):
                load_wo(n)
            sp.wait_ge(a_ready, SLOTS * PAIRS)
            sp.dma_start(rest[:, 1, 0:S], final_g.rearrange("(a n) -> a n", a=1).to_broadcast([P, S])
                         ).then_inc(fg_loaded, 16)
            for n in range(4):
                load_x(n)
            for n in range(4, 2 * KB):
                if n + 8 < 2 * KB:
                    load_wo(n + 8)
                load_x(n)

        @block.tensor
        def _(pe):
            def project(ring, bank, half, b):
                for n, (wl, hl) in enumerate(((0, 0), (0, 1), (1, 0))):
                    mm = nc.tensor.matmul(bank[:, :], w_split[:, ring, wl, b, :],
                                          hT[:, hl, b, half * HALF:(half + 1) * HALF],
                                          start=(b == 0 and n == 0), stop=(b == KB - 1 and n == 2))
                return mm

            def transpose_v(t_index, t_bank, half_index, buf):
                pe.wait_ge(stage_ready, half_index + 1)
                wait(pe, t_lo, t_index - 1)
                for b in range(GQ):
                    last = nc.tensor.transpose(t_ps[t_bank][:, b * P:(b + 1) * P],
                                               stage[:, buf, b * P:(b + 1) * P], ident[:, :])
                last.then_inc(t_done, 1)

            def transpose_x(n):
                half, b = n // KB, n % KB
                wait(pe, xt_lo, n - 3)
                for i in range(4):
                    if half and i >= 2:
                        pe.wait_ge(x_scaled_act, i - 1)
                    else:
                        pe.wait_ge(x_scaled, 4 * half + i + 1)
                    last = nc.tensor.transpose(four_banks[n % 4][:, i * P:(i + 1) * P],
                                               x_blocks[4 * half + i][:, b * P:(b + 1) * P], ident[:, :])
                last.then_inc(xt_done, 1)

            pe.wait_ge(consts_ready, 3)
            for n in range(4):
                transpose_x(n)
            for h, (kind, half) in enumerate(PROLOGUE):
                unit = "kvq".index(kind)
                wait(pe, stage_ready, h - 1)
                for b in range(KB):
                    pe.wait_ge(xt_lo, KB * half + b + 1)
                    pe.wait_ge(w_ready, 2 * unit + b // 4 + 1)
                    mm = project(unit % 2, (proj_ps, o_ps)[h % 2], half, b)
                    if h < 2 and KB * h + b + 4 < 2 * KB:
                        transpose_x(KB * h + b + 4)
                mm.then_inc(proj_done, 1)
                if h in (2, 4):
                    transpose_v(h // 2 - 1, h // 2 - 1, h - 1, 1)

            early = list(EARLY)

            def project_out(n, b):
                nh, tokens = n // KB, slice((n % KB) * P, (n % KB + 1) * P)
                at = ORDER.index(n)
                partial = n < PARTIAL_TILES and b < PAIRS - 1
                last = PAIRS - 2 if partial else KB - 1
                first = PAIRS - 1 if n < PARTIAL_TILES and not partial else 0
                if n == 0 and partial or n == ORDER[0] and b == KB - 1 or n == KB:
                    pe.wait_ge(wo_ready, n // KB * KB + b + 1)
                if n in (0, GQ) and b < PAIRS - 1:
                    pe.wait_ge(o_loaded[n // GQ][b], 32)
                if n == ORDER[0] and b == PAIRS - 1:
                    pe.wait_ge(o_lo, 2 * PAIRS)
                if b == first:
                    if n == 0 and partial:
                        pe.wait_ge(stage_ready, 2 * UNITS0 + 8 * (PAIRS - 1) + 2)
                    elif partial or at == 0:
                        pe.wait_ge(partial_sum, n)
                    elif at < BANKS:
                        pe.wait_ge(beta_ready, SLOTS * PAIRS)
                    else:
                        pe.wait_ge(y_sum, at - BANKS + 1)
                bank = proj_ps if partial else y_banks[at % BANKS]
                for m, (ol, wl) in enumerate(((0, 0), (0, 1), (1, 0))):
                    mm = nc.tensor.matmul(bank[:, :], hT[:, ol, b, tokens], w_out_of(nh, wl)[:, b, :],
                                          start=(b == first and m == 0), stop=(b == last and m == 2))
                if partial and b == last:
                    mm.then_inc(partial_done, 1)
                return mm

            def scores(p, par, s):
                hh, i = s // 8, s % 8
                width = P * (i + 1)
                if s == 0:
                    pe.wait_ge(qk_split, 4 * p + 4)
                    pe.wait_ge(k_swapped, 64 * p + 64)
                    if is_first(p):
                        pe.wait_ge(xt_lo, 2 * KB)
                wait(pe, beta_ready, SLOTS * p + s - 1)
                z = z_ps[s % 2]
                q = q_of(par, hh)[:, i * P:(i + 1) * P]
                for c in range(0, width, HALF):
                    n = max(min(width - c, HALF), 2 * P)
                    diagonal = c + HALF >= width
                    for swapped in (False, True):
                        mm = nc.tensor.matmul(z[:, c:c + n], q, k_of(par, hh, swapped)[:, c:c + n],
                                              start=not swapped, stop=swapped and not diagonal)
                mm = nc.tensor.matmul(z[:, i * P:(i + 1) * P], ident_bf[:, :], mask_bf[:, :],
                                      start=False, stop=True)
                mm.then_inc(z_ready, 1)
                if v_t_at(p, s) is not None:
                    t = v_t_at(p, s)
                    transpose_v(t_base(p) + t, t % 2, 2 * UNITS0 + 8 * p + 2 + (s == 8), int(s == 8))

            def project_part(p, s):
                half, b0, b1 = proj_part(p, s)
                unit = 0 if is_last(p) else s // 4
                if half == 0:
                    pe.wait_ge(w_ready, 2 * UNITS0 + 8 * p + 2 * unit + b0 // 4 + 1)
                if b0 == 0:
                    pe.wait_ge(stage_ready, 2 * UNITS0 + 8 * p + 2 * unit + half - (is_first(p) and s == 0))
                for b in range(b0, b1 + 1):
                    mm = project((UNITS0 + unit) % 2, proj_ps, half, b)
                if b1 == KB - 1:
                    mm.then_inc(proj_done, 1)

            def slot(p, par, s):
                if is_first(p) and s == 0:
                    project_part(p, s)
                    scores(p, par, s)
                elif not is_tail(p):
                    scores(p, par, s)
                    if s in proj_slots(p):
                        project_part(p, s)
                if isinstance(p, int):
                    for _ in range(EARLY_BY_SLOT.get((p, s), 0)):
                        project_out(*early.pop(0))
                for t, av, ahh, grp, j in av_at(p, s):
                    apar = 1 - par if s < 5 else par
                    pe.wait_ge(t_lo, t_base(p) + t + 1)
                    if j == 0:
                        group = {1: -1, 5: 0, 9: 1, 13: 2}[s]
                        wait(pe, o_summed, 4 * p + group)
                    rel = max(0, j - GQ * grp)
                    for hl in range(2):
                        if rel == GQ - 1:
                            c, moving = HALF - 2 * P, aT_pad[:, hl, :]
                        else:
                            c = rel * P
                            moving = aT[:, av % 2, hl, c:HALF]
                        mm = nc.tensor.matmul(o_ps[:, c:HALF], v_of(apar)[:, j, 2 * ahh:2 * ahh + 2, :]
                                              .rearrange("p x d -> p (x d)"), moving,
                                              start=(j == 0 and hl == 0),
                                              stop=(j == GQ * (grp + 1) - 1 and hl == 1))
                    mm.then_inc(av_done, 1)
                for t, av, thh, grp, j in units_at(p, s):
                    wait(pe, t_lo, t_base(p) + t - 1)
                    if j == 0:
                        pe.wait_ge(a_ready, SLOTS * p + (0 if s < 4 else 4 * (s // 4)))
                    for i2 in range(max(0, j - GQ * grp), GQ):
                        last = nc.tensor.transpose(t_ps[t % 2][:, i2 * P:(i2 + 1) * P],
                                                   a_g[grp][:, i2, j * P:(j + 1) * P], ident[:, :])
                    last.then_inc(t_done, 1)

            over_pairs(pe, slot, 4)

            while early:
                project_out(*early.pop(0))
            for n in ORDER:
                for b in range(PAIRS - 1 if n in [*ORDER[:BANKS], *range(PARTIAL_TILES)] else 0, KB):
                    mm = project_out(n, b)
                mm.then_inc(y_done, 1)

        @block.scalar
        def _(act):
            for b in range(0, KB, 2):
                load_x_block(act, b)
            act.wait_ge(consts_ready, 3)

            def root(cols, ready, count):
                act.wait_ge(ready, count)
                nc.scalar.activation(rstd[:, cols], ssq[:, cols], ACT.Sqrt, scale=1.0 / D,
                                     bias=eps_col[:, :]).then_inc(root_ready, 1)

            nc.scalar.activation(newton[:, 0:1], eps_col[:, :], ACT.Sqrt).then_inc(table_loaded, 1)

            def square_x(n, b):
                act.wait_ge(x_loaded[b], 16)
                wait(act, x_squared, n)
                nc.scalar.activation(oT[:, :], x_blocks[b], ACT.Square,
                                     accum_out=ssq[:, b:b + 1]).then_inc(x_squared, 1)

            def hi_x(n):
                half, b = n // KB, n % KB
                act.wait_ge(xt_done, n + 1)
                nc.scalar.activation(hT[:, 0, b, half * HALF:(half + 1) * HALF], four_banks[n % 4][:, :],
                                     ACT.Copy, scale=g_col[:, b:b + 1]).then_inc(xt_hi, 1)

            square_x(0, 0)
            square_x(1, 2)
            act.wait_ge(x_squared_dve, 2)
            root(slice(0, 4), x_squared, 2)
            for n, b in enumerate((4, 5, 6, 7)):
                square_x(2 + n, b)
            root(slice(4, 8), x_squared, 6)
            act.wait_ge(g_loaded, 16)

            def v_hi(par, half, t_index, t_bank):
                act.wait_ge(t_done, t_index + 1)
                nc.scalar.activation(v_of(par)[:, GQ * half:GQ * half + GQ, 0:4:3, :],
                                     t_ps[t_bank][:, :].rearrange("p (b x d) -> p b x d", b=GQ, x=2),
                                     ACT.Copy).then_inc(t_hi, 1)

            def to_stage(bank, h, buf):
                act.wait_ge(proj_done, h + 1)
                nc.scalar.activation(stage[:, buf, :], bank[:, :], ACT.Copy).then_inc(stage_ready, 1)

            for n in range(KB):
                if n == 4:
                    act.wait_ge(rstd_ready, 10)
                    for b in (6, 7):
                        nc.scalar.activation(x_blocks[b], x_blocks[b], ACT.Copy, scale=rstd[:, b:b + 1]
                                             ).then_inc(x_scaled_act, 1)
                hi_x(n)
            for h, (kind, half) in enumerate(PROLOGUE):
                if h in (2, 4):
                    act.wait_ge(qk_split, h // 2)
                if h in (3, 5):
                    act.wait_ge(t_done, h // 2)
                to_stage((proj_ps, o_ps)[h % 2], h, h % 2)
                if h == 0:
                    for n in range(KB, 2 * KB):
                        hi_x(n)
                if h in (3, 5):
                    v_hi(0, h // 2 - 1, h // 2 - 1, h // 2 - 1)

            def slot(p, par, s):
                evac = evac_at(p, s)
                if evac:
                    kind, half, h = evac
                    if kind == "g" and not is_last(p) or kind == "g" and s == 0:
                        act.wait_ge(qk_split, 4 * p + (4 if s == 0 else 7 + half))
                    elif kind == "v":
                        act.wait_ge(qk_split, 4 * p + 5 + half)
                    elif kind == "q":
                        act.wait_ge(t_done, t_base(p) + STEADY[8 if half else 6][0] + 1)
                    elif is_first(p):
                        act.wait_ge(qk_split, 3 + half)
                    else:
                        act.wait_ge(gate_ready, 2 * p - 1 + half)
                    to_stage(proj_ps, h, half)
                if gate_at(p, s):
                    half, number = gate_at(p, s)
                    act.wait_ge(stage_ready, evac[2] + 1)
                    wait(act, o_gated, number - 1)
                    nc.scalar.activation(gate[:, half * HALF:(half + 1) * HALF], stage[:, half, :],
                                         ACT.Sigmoid).then_inc(gate_sig, 1)
                if s % 4 == 1 and av_at(p, s - 1) and (not is_tail(p) or s < 9):
                    _, av, ohh, grp, _ = av_at(p, s - 1)[-1]
                    act.wait_ge(av_done, av_base(p) + av + 1)
                    if ohh == 0:
                        wait(act, o_lo, 2 * p - 1 + grp)
                    rows = slice(HD * ohh, HD * ohh + HD)
                    other = slice(HD - HD * ohh, 2 * HD - HD * ohh)
                    nc.scalar.activation(oT[rows, grp * HALF:(grp + 1) * HALF], o_ps[other, :],
                                         ACT.Copy).then_inc(o_shift, 1)
                for t, av, _, grp, j in (units_at(p, s - 1) if s else av_at(p, 0)):
                    rel = max(0, j - GQ * grp)
                    act.wait_ge(t_done, t_base(p) + t + 1)
                    wait(act, av_done, av_base(p) + av - 1)
                    to = aT_pad[:, 0, P:2 * P] if rel == GQ - 1 else aT[:, av % 2, 0, rel * P:HALF]
                    nc.scalar.activation(to, t_ps[t % 2][:, rel * P:HALF], ACT.Copy).then_inc(t_hi, 1)
                if s in (2, 6) and not is_first(p):
                    half = s // 4
                    act.wait_ge(o_gated, 2 * p - 1 + half)
                    if not is_tail(p):
                        wait(act, o_stored, 64 * (p - 1) + 32 * half)
                    nc.scalar.activation(split_of(p, half)[0], oT[:, half * HALF:(half + 1) * HALF],
                                         ACT.Copy).then_inc(o_hi, 1)
                if is_tail(p):
                    return
                hh, i = s // 8, s % 8
                width, grp = P * (i + 1), i // GQ
                act.wait_ge(z_ready, SLOTS * p + s + 1)
                wait(act, a_ready, SLOTS * p + s - 1)
                nc.scalar.activation(rest[:, s % 2, S - width:S], z_ps[s % 2][:, 0:width], ACT.Sigmoid,
                                     scale=-SCALE).then_inc(rest_ready, 1)
                nc.scalar.activation(a_g[grp][:, i % GQ, 0:width], z_ps[s % 2][:, 0:width], ACT.Sigmoid,
                                     scale=SCALE).then_inc(beta_ready, 1)
                if v_t_at(p, s) is not None:
                    t = v_t_at(p, s)
                    v_hi(1 - par, s // 8, t_base(p) + t, t % 2)

            over_pairs(act, slot)

            for at, n in enumerate(ORDER):
                act.wait_ge(y_sum, at + 1)
                wait(act, y_squared, at)
                nc.scalar.activation(rest[:, 0, 0:HALF], y_of(n), ACT.Square, accum_out=ssq[:, n:n + 1]
                                     ).then_inc(y_squared, 1)
                if n >= KB:
                    b = n - KB
                    root(slice(b, b + 1), ssq_summed, b + 1)
                    for half in range(2):
                        act.wait_ge(out_ready, 2 * b + half + 1)
                        cols = slice(half * HALF, (half + 1) * HALF)
                        act.dma_start(out[b * P:(b + 1) * P, cols], out_of(b)[half]).then_inc(stored[b % 2], 16)
            for odd in range(2):
                act.wait_ge(stored[odd], 16 * KB)

        @block.vector
        def _(dve):
            def split_hi_w(ring, part):
                nc.vector.tensor_copy(w_split[:, ring, 0, 4 * part:4 * part + 4, :],
                                      w_raw[:, part, :].rearrange("p (b n) -> p b n", b=4)).then_inc(w_hi, 1)

            def rsqrt(cols, n):
                r, m, t = rstd[:, cols], mean_sq[:, cols], newton[:, cols]
                nc.vector.tensor_scalar(m, ssq[:, cols], 1.0 / D, EPS, ALU.mult, ALU.add).then_inc(mean_ready, 1)
                dve.wait_ge(root_ready, n + 1)
                nc.vector.reciprocal(r, r).then_inc(rstd_ready, 1)
                dve.wait_ge(mean_ready, n + 1)
                dve.wait_ge(rstd_ready, 5 * n + 1)
                nc.vector.tensor_tensor(t, r, r, ALU.mult).then_inc(rstd_ready, 1)
                dve.wait_ge(rstd_ready, 5 * n + 2)
                nc.vector.tensor_tensor(t, t, m, ALU.mult).then_inc(rstd_ready, 1)
                dve.wait_ge(rstd_ready, 5 * n + 3)
                nc.vector.tensor_scalar(t, t, -0.5, 1.5, ALU.mult, ALU.add).then_inc(rstd_ready, 1)
                dve.wait_ge(rstd_ready, 5 * n + 4)
                nc.vector.tensor_tensor(r, r, t, ALU.mult).then_inc(rstd_ready, 1)
                dve.wait_ge(rstd_ready, 5 * n + 5)

            nc.vector.memset(aT_pad[:, :, 0:P].bitcast(F32), 0.0)
            nc.vector.memset(eps_col[:, :], EPS)
            nc.vector.memset(rest[:, :, S:S + 1], 1.0).then_inc(consts_ready, 1)
            def square_x(n, b):
                dve.wait_ge(x_loaded[b], 16)
                wait(dve, x_squared_dve, n)
                nc.vector.tensor_tensor_reduce(gate[:, :], x_blocks[b], x_blocks[b], 1.0, 0.0, ALU.mult, ALU.add,
                                               ssq[:, b:b + 1]).then_inc(x_squared_dve, 1)

            def scale_x(blocks):
                for b in blocks:
                    nc.vector.tensor_scalar(x_blocks[b], x_blocks[b], rstd[:, b:b + 1], None,
                                            ALU.mult).then_inc(x_scaled, 1)

            def lo_x(n):
                half, b = n // KB, n % KB
                cols = slice(half * HALF, (half + 1) * HALF)
                dve.wait_ge(xt_hi, n + 1)
                nc.vector.scalar_tensor_tensor(hT[:, 1, b, cols], four_banks[n % 4][:, :], g_col[:, b:b + 1],
                                               hT[:, 0, b, cols].bitcast(F32), ALU.mult, ALU.subtract
                                               ).then_inc(xt_lo, 1)

            def next_w(n):
                dve.wait_ge(w_loaded[n % 2], 16 * (n // 2 + 1))
                split_hi_w((n // 2) % 2, n % 2)

            square_x(0, 1)
            square_x(1, 3)
            dve.wait_ge(table_loaded, 1)
            dve.wait_ge(x_squared_dve, 2)
            dve.wait_ge(x_squared, 2)
            rsqrt(slice(0, 4), 0)
            scale_x(range(4))
            next_w(0)
            next_w(1)
            dve.wait_ge(x_squared, 6)
            rsqrt(slice(4, 8), 1)
            dve.wait_ge(g_loaded, 16)
            for n in range(KB):
                lo_x(n)
                if n == 3:
                    scale_x((4, 5))
                if n in (5, 7):
                    next_w(n // 2)

            def split_heads(kind, par, half, h, buf, count):
                dve.wait_ge(stage_ready, h + 1)
                cols = slice(half * HALF, (half + 1) * HALF)
                for hh in range(2):
                    rows = slice(HD * hh, HD * hh + HD)
                    to = q_of(par, hh) if kind == "q" else k_of(par, hh, False)
                    last = nc.vector.tensor_copy(to[rows, cols], stage[rows, buf, :])
                last.then_inc(qk_hi, 1)
                dve.wait_ge(qk_hi, count)
                for hh in range(2):
                    rows = slice(HD * hh, HD * hh + HD)
                    other = slice(HD - HD * hh, 2 * HD - HD * hh)
                    to = q_of(par, hh) if kind == "q" else k_of(par, hh, False)
                    last = nc.vector.tensor_tensor(to[other, cols], stage[rows, buf, :],
                                                   to[rows, cols].bitcast(F32), ALU.subtract)
                last.then_inc(qk_split, 1)

            def v_lo(par, half, t_index, t_bank):
                dve.wait_ge(t_hi, t_index + 1)
                blocks = slice(GQ * half, GQ * half + GQ)
                nc.vector.tensor_tensor(v_of(par)[:, blocks, 1:3, :],
                                        t_ps[t_bank][:, :].rearrange("p (b x d) -> p b x d", b=GQ, x=2),
                                        v_of(par)[:, blocks, 0:4:3, :].bitcast(F32), ALU.subtract
                                        ).then_inc(t_lo, 1)

            for n in range(KB, 2 * KB):
                lo_x(n)
                if n == KB + 2:
                    split_heads("k", 0, 0, 0, 0, 1)
            for h, (kind, half) in enumerate(PROLOGUE):
                if h in (2, 4, 5):
                    split_heads(kind, 0, half, h, h % 2, {2: 2, 4: 3, 5: 4}[h])
                if h in (3, 5):
                    v_lo(0, h // 2 - 1, h // 2 - 1, h // 2 - 1)
                if h in (2, 3):
                    dve.wait_ge(proj_done, h + 1)
                    next_w(2 * h)
                    next_w(2 * h + 1)

            def wo_hi_part(n):
                dve.wait_ge(wo_loaded[n % WO_RING], 16 * (n // WO_RING + 1))
                dve.wait_ge(av_done, AV_PER_PAIR * (PAIRS - 1 + n // KB))
                nc.vector.tensor_copy(w_out_of(n // KB, 0)[:, n % KB, :], wo_raw[:, n % WO_RING, :]).then_inc(wo_hi, 1)

            def slot(p, par, s):
                evac = evac_at(p, s)
                if evac:
                    kind, half, h = evac
                    if kind in "kq":
                        split_heads(kind, 1 - par, half, h, half,
                                    4 * p + 5 + half + (2 if kind == "q" else 0))
                if gate_at(p, s):
                    half, number = gate_at(p, s)
                    dve.wait_ge(gate_sig, number + 1)
                    cols = slice(half * HALF, (half + 1) * HALF)
                    nc.vector.tensor_tensor(gate[:, cols], stage[:, half, :], gate[:, cols], ALU.mult
                                            ).then_inc(gate_ready, 1)
                if s % 4 == 1 and av_at(p, s - 1) and (not is_tail(p) or s < 9):
                    _, _, ohh, grp, _ = av_at(p, s - 1)[-1]
                    group = {1: -1, 5: 0, 9: 1, 13: 2}[s]
                    dve.wait_ge(o_shift, 4 * p + group)
                    rows = slice(HD * ohh, HD * ohh + HD)
                    cols = slice(grp * HALF, (grp + 1) * HALF)
                    nc.vector.tensor_tensor(oT[rows, cols], o_ps[rows, :], oT[rows, cols], ALU.add
                                            ).then_inc(o_summed, 1)
                for t, av, _, grp, j in (units_at(p, s - 1) if s else av_at(p, 0)):
                    rel = max(0, j - GQ * grp)
                    dve.wait_ge(t_hi, t_base(p) + t + 1)
                    if rel == GQ - 1:
                        hi, lo = aT_pad[:, 0, P:2 * P], aT_pad[:, 1, P:2 * P]
                    else:
                        hi, lo = aT[:, av % 2, 0, rel * P:HALF], aT[:, av % 2, 1, rel * P:HALF]
                    nc.vector.tensor_tensor(lo, t_ps[t % 2][:, rel * P:HALF], hi.bitcast(F32), ALU.subtract
                                            ).then_inc(t_lo, 1)
                if s in (2, 6) and not is_first(p):
                    half = s // 4
                    dve.wait_ge(o_hi, 2 * p - 1 + half)
                    hi, lo = split_of(p, half)
                    nc.vector.tensor_tensor(lo, oT[:, half * HALF:(half + 1) * HALF], hi.bitcast(F32),
                                            ALU.subtract).then_inc(o_lo, 1)
                if is_tail(p):
                    return
                width = P * (s % 8 + 1)
                span = rest[:, s % 2, S - 1:(S - 1 - width if width < S else None):-1]
                dve.wait_ge(rest_ready, SLOTS * p + s + 1)
                nc.vector.tensor_tensor_scan(span, span, span, 1.0, ALU.mult, ALU.bypass
                                             ).then_inc(scan_done, 1)
                if v_t_at(p, s) is not None:
                    t = v_t_at(p, s)
                    v_lo(1 - par, s // 8, t_base(p) + t, t % 2)
                if s % 4 in (1, 2) and not is_last(p):
                    part = s % 4 - 1
                    unit = UNITS0 + 4 * p + s // 4 + 1
                    dve.wait_ge(proj_done, 2 * unit - 2)
                    dve.wait_ge(w_loaded[part], 16 * unit + 16)
                    split_hi_w((UNITS0 + 1 + s // 4) % 2, part)
                if is_last(p):
                    for n in WO_BY_SLOT.get(s, ()):
                        wo_hi_part(n)
                        dve.wait_ge(wo_hi, n + 1)
                        wo_lo_part(nc.vector, n)
                if is_last(p) and s in PARTIAL_SLOTS:
                    n = PARTIAL_SLOTS.index(s)
                    dve.wait_ge(partial_done, n + 1)
                    dve.wait_ge(xs_loaded[n], 16)
                    nc.vector.tensor_tensor(stage[:, n, :], proj_ps[:, :], stage[:, n, :], ALU.add
                                            ).then_inc(partial_sum, 1)

            over_pairs(dve, slot)

            for at, n in enumerate(ORDER):
                b = n % KB
                for block in WO_BY_TILE.get(at, ()):
                    wo_hi_part(KB + block)
                dve.wait_ge(y_done, at + 1)
                if n < PARTIAL_TILES:
                    addend = stage[:, n, :]
                else:
                    dve.wait_ge(xr_loaded[at % 4], 16 * X_COUNT[at])
                    addend = a_g[0][:, at % 4, :]
                if n >= KB:
                    wait(dve, y_squared, n - 1)
                    if n >= KB + 2:
                        dve.wait_ge(out_ready, 2 * (n - KB) - 2)
                nc.vector.tensor_tensor(y_of(n), y_banks[at % BANKS][:, :], addend, ALU.add
                                        ).then_inc(y_sum, 1)
                if n < KB:
                    continue
                if b == 0:
                    dve.wait_ge(fg_loaded, 16)
                dve.wait_ge(y_squared, n + 1)
                nc.vector.tensor_tensor(ssq[:, b:b + 1], ssq[:, b:b + 1], ssq[:, n:n + 1], ALU.add
                                        ).then_inc(ssq_summed, 1)
                dve.wait_ge(ssq_summed, b + 1)
                for half in range(2):
                    nc.vector.tensor_tensor(y_of(b + KB * half), y_of(b + KB * half),
                                            rest[:, 1, half * HALF:(half + 1) * HALF], ALU.mult
                                            ).then_inc(y_weighted, 1)
                rsqrt(slice(b, b + 1), 2 + b)
                dve.wait_ge(y_weighted, 2 * b + 2)
                wait(dve, stored[b % 2], 32 * (b // 2))
                for half in range(2):
                    nc.vector.tensor_scalar(out_of(b)[half], y_of(b + KB * half), rstd[:, b:b + 1], None,
                                            ALU.mult).then_inc(out_ready, 1)

        @block.gpsimd
        def _(pool):
            pool.dma_start(g_col[:, :], norm_g).then_inc(g_loaded, 16)
            nc.gpsimd.memset(ident[:, :], 0.0)
            nc.gpsimd.memset(mask_bf[:, :], 0.0)
            nc.gpsimd.memset(ident_bf[:, :], 0.0).then_inc(zeros_ready, 1)
            pool.wait_ge(zeros_ready, 1)
            for t in (ident, ident_bf):
                last = nc.gpsimd.affine_select(out=t[:, :], in_=t[:, :], compare_op=ALU.not_equal, fill=1.0,
                                               base=0, pattern=[[-1, P]], channel_multiplier=1)
            nc.gpsimd.affine_select(out=mask_bf[:, :], in_=mask_bf[:, :], compare_op=ALU.is_gt, fill=MASKED,
                                    base=0, pattern=[[-1, P]], channel_multiplier=1).then_inc(consts_ready, 2)

            def lo_w(n, ring, part):
                pool.wait_ge(w_hi, n + 1)
                to = w_split[:, ring, :, 4 * part:4 * part + 4, :]
                nc.gpsimd.tensor_tensor(to[:, 1], w_raw[:, part, :].rearrange("p (b n) -> p b n", b=4),
                                        to[:, 0].bitcast(F32), ALU.subtract).then_inc(w_ready, 1)

            for n in range(2 * UNITS0 + 2):
                lo_w(n, (n // 2) % 2, n % 2)

            def slot(p, par, s):
                if s in (1, 5) and not is_first(p):
                    half = s // 4
                    pool.wait_ge(o_summed, 4 * p - 1 + half)
                    pool.wait_ge(gate_ready, 2 * p - 1 + half)
                    cols = slice(half * HALF, (half + 1) * HALF)
                    nc.gpsimd.tensor_tensor(oT[:, cols], oT[:, cols], gate[:, cols], ALU.mult
                                            ).then_inc(o_gated, 1)
                if is_tail(p):
                    return
                i = s % 8
                width = P * (i + 1)
                a = a_g[i // GQ][:, i % GQ, 0:width]
                pool.wait_ge(beta_ready, SLOTS * p + s + 1)
                pool.wait_ge(scan_done, SLOTS * p + s + 1)
                nc.gpsimd.tensor_tensor(a, a, rest[:, s % 2, S + 1 - width:S + 1], ALU.mult
                                        ).then_inc(a_ready, 1)
                if s % 4 in (1, 2) and not is_last(p):
                    n = 2 * (UNITS0 + 4 * p + s // 4 + 1) + s % 4 - 1
                    lo_w(n, (UNITS0 + 1 + s // 4) % 2, s % 4 - 1)

            over_pairs(pool, slot)

            for n in range(KB, 2 * KB):
                pool.wait_ge(wo_hi, n + 1)
                wo_lo_part(nc.gpsimd, n)


def kernel(**inputs):
    import numpy as _np
    import concourse.bacc as _bacc
    from concourse.bass_utils import run_bass_kernel_spmd as _run

    nc = _bacc.Bacc("TRN2", target_bir_lowering=False, num_devices=1)
    arrays = {
        "x": inputs["x"].reshape(S, D),
        "norm_g": inputs["norm_g"].reshape(KB, P).T,
        "w_in": inputs["sb_w_in"].reshape(2, GQ, P, 4 * KB, P).transpose(3, 0, 2, 1, 4)
                                 .reshape(4 * KB, 2, P, HALF),
        "w_out": inputs["sb_w_out"].reshape(D, D),
        "final_g": inputs["final_g"].reshape(D),
    }
    arrays = {name: _np.ascontiguousarray(a) for name, a in arrays.items()}
    aps = {name: nc.dram_tensor(name, a.shape, F32, kind="ExternalInput").ap() for name, a in arrays.items()}
    out = nc.dram_tensor("out", [S, D], F32, kind="ExternalOutput").ap()
    stick_breaking_layer(nc, aps["x"], aps["norm_g"], aps["w_in"], aps["w_out"], aps["final_g"], out)
    r = _run(nc, [arrays], core_ids=[0])
    return r.results[0]["out"].reshape(1, S, D)
```

```python
from contextlib import ExitStack

import concourse.bass as bass
from concourse import mybir

ALU = mybir.AluOpType
ACT = mybir.ActivationFunctionType
F32 = mybir.dt.float32
F32R = mybir.dt.float32r

P = 128
D = 1024
S = 1024
HEADS = 16
HD = D // HEADS
PAIRS = HEADS // 2
KB = D // P
HALF = 512
GQ = HALF // P
SLOTS = 16
EPS = 1e-6
SCALE = HD ** -0.5

UNITS0 = 3
T_PER_PAIR, AV_PER_PAIR = 26, 24


def plan(with_v):
    out, t, av = [], 0, 0
    for s in range(SLOTS):
        v_t = None
        if with_v and s in (6, 8):
            v_t, t = t, t + 1
        hh, grp = ((1, 1), (0, 0), (0, 1), (1, 0))[s // 4]
        blocks = (2 * (s % 4), 2 * (s % 4) + 1) if grp else (s % 4,)
        units = []
        for j in blocks:
            units.append((t, av, hh, grp, j))
            t, av = t + 1, av + 1
        out.append((v_t, units))
    return out


STEADY, LAST = plan(True), plan(False)
FIRST_SKIPS = 8


def t_base(p):
    if isinstance(p, int) and p == PAIRS:
        return t_base(PAIRS - 1) + T_PER_PAIR - 2
    return T_PER_PAIR * p + (2 - FIRST_SKIPS)


def av_base(p):
    return AV_PER_PAIR * p - FIRST_SKIPS


def is_last(p):
    return isinstance(p, int) and p == PAIRS - 1


def is_tail(p):
    return isinstance(p, int) and p == PAIRS


def is_first(p):
    return isinstance(p, int) and p == 0


def wait(eng, sem, value):
    if not isinstance(value, int) or value > 0:
        eng.wait_ge(sem, value)


def units_at(p, s):
    if isinstance(p, int) and (p == 0 and s < 4 or p == PAIRS and s >= 4):
        return []
    return (LAST if isinstance(p, int) and p >= PAIRS - 1 else STEADY)[s][1]


def av_at(p, s):
    if s > 0:
        return units_at(p, s - 1)
    return [] if is_first(p) else [(-1, -1, 1, 0, GQ - 1)]


def v_t_at(p, s):
    return None if isinstance(p, int) and p >= PAIRS - 1 else STEADY[s][0]


def proj_slots(p):
    return range(SLOTS // 2) if is_last(p) else range(SLOTS)


def proj_part(p, s):
    if is_last(p):
        return s // 4, 2 * (s % 4), 2 * (s % 4) + 1
    return (s % 4) // 2, 4 * (s % 2), 4 * (s % 2) + 3


def evac_at(p, s):
    if s % 2 or is_tail(p) or (is_first(p) and s == 0):
        return None
    number = 2 * UNITS0 + 8 * p + s // 2 - 1
    if s == 0:
        return "g", 1, number
    if is_last(p):
        return ("g", s // 4 - 1, 2 * UNITS0 + 8 * p + s // 4 - 1) if s in (4, 8) else None
    return "kvqg"[(s - 1) // 4], ((s - 1) % 4) // 2, number


def gate_at(p, s):
    evac = evac_at(p, s)
    if not evac or evac[0] != "g":
        return None
    return evac[1], 2 * p - 1 if s == 0 else 2 * p + evac[1]


PROLOGUE = (("k", 0), ("v", 0), ("k", 1), ("v", 1), ("q", 0), ("q", 1))
X_ACT, X_DVE = (3, 6, 7), (0, 1, 2, 4, 5)
X_SCALED = [(1, X_ACT.index(b) + 1) if b in X_ACT else (0, X_DVE.index(b) + 1) for b in range(KB)]
WARM_UP = 34
BANKS = 5
PARTIAL_TILES = 2
ORDER = [*range(PARTIAL_TILES, KB), *range(PARTIAL_TILES), *range(KB, 2 * KB)]
EARLY = [(n, b) for n in [*range(PARTIAL_TILES), *ORDER[:BANKS]] for b in range(PAIRS - 1)]
EARLY_BY_SLOT = {(PAIRS - 1, s): n for s, n in zip(range(8, 16), (2, 2, 2, 1, 4, 3, 3, 3))}
EARLY_BY_SLOT |= {(PAIRS, s): 4 for s in range(5)}
X_COUNT = [sum(ORDER[m] >= PARTIAL_TILES for m in range(at % 4, at + 1, 4)) for at in range(2 * KB)]
PARTIAL_SLOTS = (11, 13)
WO_RING = 4
WO_BY_SLOT = {5: (0,), 6: (1,), 7: (2,), 8: (3,), 9: (4, 5), 10: (6,), 12: (7,)}
WO_BY_TILE = {0: (0, 1), 1: (2,), 2: (3,), 3: (4,), 4: (5,), 5: (6, 7)}


def z_offset(i):
    return 2 * P if P * (i + 1) == HALF + P else 0


def stick_breaking_layer(nc, x, norm_g, w_in, w_out, final_g, out):
    o_hi_dram = nc.dram_tensor("o_hi_scratch", [PAIRS - 1, P, S], F32).ap()
    o_lo_dram = nc.dram_tensor("o_lo_scratch", [PAIRS - 1, P, S], F32).ap()

    with ExitStack() as ctx:
        def sb(name, shape, dt=F32):
            return ctx.enter_context(nc.sbuf_tensor(name, shape, dt))

        def ps(name, shape, dt=F32):
            return ctx.enter_context(nc.psum_tensor(name, shape, dt))

        def sem(name):
            return ctx.enter_context(nc.semaphore(name))

        hT = sb("hT", [P, 2, KB, S], F32R)
        arena = sb("arena", [P, 2, 4, 2 * S], F32R)
        w_raw = sb("w_raw", [P, 2, HALF])
        a_g = [sb("a_group0", [P, GQ, HALF]), sb("a_group1", [P, GQ, S])]
        rest = sb("rest", [P, 2, S + 1])
        aT = sb("aT", [P, 2, 2, HALF], F32R)
        aT_pad = sb("aT_pad", [P, 2, 2 * P], F32R)
        stage = sb("stage", [P, 2, HALF])
        gate = sb("gate", [P, S])
        oT = sb("oT", [P, S])
        o_split = sb("o_split", [P, 2, HALF], F32R)
        ident = sb("ident", [P, P])
        before = sb("before", [P, P])
        not_before = sb("not_before", [P, P])
        g_col = sb("g_col", [P, KB])
        ssq = sb("ssq", [P, 2 * KB])
        rstd = sb("rstd", [P, KB])
        mean_sq = sb("mean_sq", [P, KB])
        newton = sb("newton", [P, KB])
        eps_col = sb("eps_col", [P, 1])
        with nc.sbuf_tensor("w_split", [P, 2, 2, KB, P], F32R) as w_split:
            pass
        wo_raw = sb("wo_raw", [P, WO_RING, HALF])

        x_blocks = ([a_g[1][:, b, :] for b in range(4)]
                    + [a_g[0][:, 2 * b:2 * b + 2, :].rearrange("p a n -> p (a n)") for b in range(2)]
                    + [rest[:, b, 0:S] for b in range(2)])

        def q_of(par, hh):
            return arena[:, par, 0, hh * S:(hh + 1) * S]

        def k_of(par, hh, swapped):
            return arena[:, par, 2 if swapped else 1, hh * S:(hh + 1) * S]

        def v_of(par):
            return arena[:, par, 3, :].rearrange("p (b x d) -> p b x d", b=KB, x=4)

        def w_out_of(half, hl):
            return arena[:, half, 2 * hl:2 * hl + 2, :].rearrange("p a (b n) -> p (a b) n", n=HALF)

        z_ps = [ps(f"z_ps{b}", [P, S]) for b in range(2)]
        t_ps = [ps(f"t_ps{b}", [P, HALF]) for b in range(2)]
        proj_ps = ps("proj_ps", [P, HALF])
        o_ps = ps("o_ps", [P, HALF])
        z_banks = [z[:, c:c + HALF] for z in z_ps for c in (0, HALF)]
        y_banks = [proj_ps] + z_banks

        x_loaded = [sem(f"x_loaded{b}") for b in range(KB)]
        g_loaded = sem("g_loaded")
        consts_ready = sem("consts_ready")
        x_squared = sem("x_squared")
        mean_ready = sem("mean_ready")
        root_ready = sem("root_ready")
        rstd_ready = sem("rstd_ready")
        x_scaled = sem("x_scaled")
        x_scaled_act = sem("x_scaled_act")
        xt_done = sem("xt_done")
        xt_hi = sem("xt_hi")
        xt_lo = sem("xt_lo")
        w_loaded = [sem(f"w_loaded{b}") for b in range(2)]
        w_hi = sem("w_hi")
        w_ready = sem("w_ready")
        proj_done = sem("proj_done")
        stage_ready = sem("stage_ready")
        qk_hi = sem("qk_hi")
        qk_split = sem("qk_split")
        gate_sig = sem("gate_sig")
        gate_ready = sem("gate_ready")
        k_swapped = sem("k_swapped")
        z_ready = sem("z_ready")
        rest_ready = sem("rest_ready")
        beta_ready = sem("beta_ready")
        rest_masked = sem("rest_masked")
        beta_masked = sem("beta_masked")
        scan_done = sem("scan_done")
        a_ready = sem("a_ready")
        t_done = sem("t_done")
        t_hi = sem("t_hi")
        t_lo = sem("t_lo")
        av_done = sem("av_done")
        o_shift = sem("o_shift")
        o_summed = sem("o_summed")
        o_gated = sem("o_gated")
        o_hi = sem("o_hi")
        o_lo = sem("o_lo")
        o_stored = sem("o_stored")
        o_loaded = [[sem(f"o_loaded{half}_{b}") for b in range(PAIRS - 1)] for half in range(2)]
        wo_loaded = [sem(f"wo_loaded{b}") for b in range(WO_RING)]
        wo_hi = sem("wo_hi")
        wo_ready = sem("wo_ready")
        xs_loaded = [sem(f"xs_loaded{n}") for n in range(PARTIAL_TILES)]
        partial_done = sem("partial_done")
        partial_sum = sem("partial_sum")
        y_done = sem("y_done")
        y_sum = sem("y_sum")
        y_squared = sem("y_squared")
        ssq_summed = sem("ssq_summed")
        y_weighted = sem("y_weighted")
        zeros_ready = sem("zeros_ready")
        xr_loaded = [sem(f"xr_loaded{b}") for b in range(4)]
        fg_loaded = sem("fg_loaded")
        out_ready = sem("out_ready")
        out_ready_act = sem("out_ready_act")
        stored = [sem(f"stored{b}") for b in range(2)]
        table_loaded = sem("table_loaded")
        x_squared_dve = sem("x_squared_dve")

        block = ctx.enter_context(nc.Block())

        def wait_wo(eng, n):
            eng.wait_ge(wo_loaded[n % WO_RING], 16 * (n // WO_RING + 1))
            eng.wait_ge(av_done, AV_PER_PAIR * (PAIRS - 1 + n // KB))

        def wo_lo_part(engine, n):
            engine.tensor_tensor(w_out_of(n // KB, 1)[:, n % KB, :], wo_raw[:, n % WO_RING, :],
                                 w_out_of(n // KB, 0)[:, n % KB, :].bitcast(F32), ALU.subtract
                                 ).then_inc(wo_ready, 1)

        y_half = a_g[1][:, :, :].rearrange("p a (b n) -> p (a b) n", b=2)

        def y_of(n):
            return y_half[:, n, :] if n < KB else gate[:, (n % 2) * HALF:(n % 2 + 1) * HALF]

        def out_of(b):
            return [stage[:, 0, :], stage[:, 1, :]] if b % 2 else [oT[:, 0:HALF], oT[:, HALF:S]]

        def split_of(p, half):
            if is_tail(p):
                cols = slice(half * HALF, (half + 1) * HALF)
                return hT[:, 0, PAIRS - 1, cols], hT[:, 1, PAIRS - 1, cols]
            return o_split[:, 0, :], o_split[:, 1, :]

        def load_x_block(eng, b):
            eng.dma_start(x_blocks[b], x[b * P:(b + 1) * P, :]).then_inc(x_loaded[b], 16)

        def over_pairs(eng, slot, last_slot=6):
            for s in range(SLOTS):
                slot(0, 0, s)
            with eng.Fori(0, (PAIRS - 2) // 2) as two:
                for odd in range(2):
                    for s in range(SLOTS):
                        slot(two * 2 + (1 + odd), 1 - odd, s)
            for s in range(SLOTS):
                slot(PAIRS - 1, 1, s)
            for s in range(last_slot + 1):
                slot(PAIRS, 0, s)

        @block.sync
        def _(sp):
            wo_v = w_out.rearrange("(b p) n -> b p n", p=P)

            def load_w(n, half, buf, columns):
                wait(sp, w_ready, n - 1)
                sp.dma_start(w_raw[:, buf, :], w_in[bass.ds(columns, 1), half, :, :]
                             .rearrange("a p n -> (a p) n")).then_inc(w_loaded[buf], 16)

            def swap_k(p, par):
                sp.wait_ge(qk_split, 4 * p + 2)
                wait(sp, z_ready, SLOTS * p - SLOTS)
                for hh in range(2):
                    for to in range(2):
                        sp.dma_start(k_of(par, hh, True)[HD * to:HD * to + HD, :].bitcast(F32),
                                     k_of(par, hh, False)[HD * (1 - to):HD * (1 - to) + HD, :].bitcast(F32)
                                     ).then_inc(k_swapped, 16)

            for b in (1, 3):
                load_x_block(sp, b)
            kinds = (1, 2, 0)
            for n in range(2 * UNITS0):
                load_w(n, n % 2, n % 2, kinds[n // 2] * KB)
                if n == 1:
                    for b in (5, 7):
                        load_x_block(sp, b)
            for half in range(2):
                load_w(2 * UNITS0 + half, half, half, KB + 1)
            swap_k(0, 0)

            def slot(p, par, s):
                if s % 4 < 2 and not (isinstance(p, int) and p >= PAIRS - 1):
                    m = s // 4
                    columns = p + (2 * KB + 1, 1, 3 * KB, KB + 2)[m]
                    load_w(2 * (UNITS0 + 1 + m) + 8 * p + s % 4, s % 4, s % 4, columns)
                if s in (3, 7) and not is_first(p) and not is_tail(p):
                    half = s // 4
                    sp.wait_ge(o_lo, 2 * p - 1 + half)
                    for dram, hl in ((o_hi_dram, 0), (o_lo_dram, 1)):
                        sp.dma_start(dram[bass.ds(p - 1, 1), :, half * HALF:(half + 1) * HALF]
                                     .rearrange("a p n -> (a p) n"),
                                     o_split[:, hl, :].bitcast(F32)).then_inc(o_stored, 16)
                if s == 5 and not (isinstance(p, int) and p >= PAIRS - 1):
                    swap_k(p + 1, 1 - par)

            for s in range(SLOTS):
                slot(0, 0, s)
            with sp.Fori(0, (PAIRS - 4) // 2) as two:
                for odd in range(2):
                    for s in range(SLOTS):
                        slot(two * 2 + (1 + odd), 1 - odd, s)
            for p in (PAIRS - 3, PAIRS - 2):
                for s in range(SLOTS):
                    if p == PAIRS - 2 and s in (12, 13):
                        n = 2 * UNITS0 + 8 * (PAIRS - 1) + s % 4
                        load_w(n, s % 4, s % 4, 3 * KB + PAIRS - 1)
                    else:
                        slot(p, p % 2, s)

            def load_wo(n):
                if n == 0:
                    sp.wait_ge(proj_done, 2 * UNITS0 + 8 * (PAIRS - 1))
                wait(sp, wo_ready, n - WO_RING + 1)
                sp.dma_start(wo_raw[:, n % WO_RING, :], wo_v[n % KB, :, (n // KB) * HALF:(n // KB + 1) * HALF]
                             ).then_inc(wo_loaded[n % WO_RING], 16)

            def load_o(half, b):
                cols = slice(half * HALF, (half + 1) * HALF)
                for dram, hl in ((o_hi_dram, 0), (o_lo_dram, 1)):
                    sp.dma_start(hT[:, hl, b, cols].bitcast(F32), dram[b, :, cols]).then_inc(o_loaded[half][b], 16)

            for n in range(WO_RING):
                load_wo(n)
            slot(PAIRS - 1, 1, 3)
            sp.wait_ge(proj_done, 2 * UNITS0 + 8 * (PAIRS - 1) + 1)
            sp.wait_ge(o_stored, 64 * (PAIRS - 2))
            load_o(0, 0)
            load_o(0, 1)
            load_wo(4)
            load_o(0, 2)
            load_wo(5)
            load_o(0, 3)
            slot(PAIRS - 1, 1, 7)
            load_wo(6)
            load_o(0, 4)
            load_o(0, 5)
            load_wo(7)
            sp.wait_ge(o_stored, 64 * (PAIRS - 1))
            load_o(0, PAIRS - 2)
            for n in range(PARTIAL_TILES):
                sp.wait_ge(gate_ready, 2 * PAIRS - 1 + n)
                sp.dma_start(stage[:, n, :], x[n * P:(n + 1) * P, 0:HALF]).then_inc(xs_loaded[n], 16)
            sp.wait_ge(proj_done, 2 * UNITS0 + 8 * (PAIRS - 1) + 2)
            for b in range(PAIRS - 1):
                load_o(1, b)

            def load_x(n):
                wait(sp, y_sum, n - 3)
                if n == 0:
                    sp.wait_ge(t_done, t_base(PAIRS))
                if ORDER[n] < PARTIAL_TILES:
                    return
                b, nh = ORDER[n] % KB, ORDER[n] // KB
                sp.dma_start(a_g[0][:, n % 4, :], x[b * P:(b + 1) * P, nh * HALF:(nh + 1) * HALF]
                             ).then_inc(xr_loaded[n % 4], 16)

            for n in range(KB, KB + WO_RING):
                load_wo(n)
            sp.wait_ge(a_ready, SLOTS * PAIRS)
            sp.dma_start(rest[:, 1, 0:S], final_g.rearrange("(a n) -> a n", a=1).to_broadcast([P, S])
                         ).then_inc(fg_loaded, 16)
            for n in range(4):
                load_x(n)
            for n in range(4, 2 * KB):
                if n + 8 < 2 * KB:
                    load_wo(n + 8)
                load_x(n)
            sp.wait_ge(out_ready, KB)
            sp.dma_start(out[S - P:S, HALF:S], out_of(KB - 1)[1]).then_inc(stored[(KB - 1) % 2], 16)

        @block.tensor
        def _(pe):
            def project(ring, bank, half, b):
                for n, (wl, hl) in enumerate(((0, 0), (0, 1), (1, 0))):
                    mm = nc.tensor.matmul(bank[:, :], w_split[:, ring, wl, b, :],
                                          hT[:, hl, b, half * HALF:(half + 1) * HALF],
                                          start=(b == 0 and n == 0), stop=(b == KB - 1 and n == 2))
                return mm

            def transpose_v(t_index, t_bank, half_index, buf):
                pe.wait_ge(stage_ready, half_index + 1)
                wait(pe, t_lo, t_index - 1)
                for b in range(GQ):
                    last = nc.tensor.transpose(t_ps[t_bank][:, b * P:(b + 1) * P],
                                               stage[:, buf, b * P:(b + 1) * P], ident[:, :])
                last.then_inc(t_done, 1)

            def transpose_x(n):
                half, b = n // KB, n % KB
                wait(pe, xt_lo, n - 3)
                for i in range(4):
                    scaled, count = X_SCALED[4 * half + i]
                    pe.wait_ge((x_scaled, x_scaled_act)[scaled], count)
                    last = nc.tensor.transpose(z_banks[n % 4][:, i * P:(i + 1) * P],
                                               x_blocks[4 * half + i][:, b * P:(b + 1) * P], ident[:, :])
                last.then_inc(xt_done, 1)

            pe.wait_ge(consts_ready, 4)
            pe.wait_ge(x_squared, 1)
            for n in range(WARM_UP):
                nc.tensor.transpose(z_banks[0][:, 0:P], ident[:, :], ident[:, :])
            for n in range(4):
                transpose_x(n)
            for h, (kind, half) in enumerate(PROLOGUE):
                unit = "kvq".index(kind)
                wait(pe, stage_ready, h - 1)
                for b in range(KB):
                    pe.wait_ge(xt_lo, KB * half + b + 1)
                    pe.wait_ge(w_ready, 2 * unit + b // 4 + 1)
                    mm = project(unit % 2, (proj_ps, o_ps)[h % 2], half, b)
                    if h == 0 and b < 4:
                        transpose_x(b + 4)
                    if h == 1:
                        transpose_x(KB + b)
                mm.then_inc(proj_done, 1)
                if h in (2, 4):
                    transpose_v(h // 2 - 1, h // 2 - 1, h - 1, 1)

            early = list(EARLY)

            def project_out(n, b):
                nh, tokens = n // KB, slice((n % KB) * P, (n % KB + 1) * P)
                at = ORDER.index(n)
                partial = n < PARTIAL_TILES and b < PAIRS - 1
                last = PAIRS - 2 if partial else KB - 1
                first = PAIRS - 1 if n < PARTIAL_TILES and not partial else 0
                if n == 0 and partial or n == ORDER[0] and b == KB - 1 or n == KB:
                    pe.wait_ge(wo_ready, n // KB * KB + b + 1)
                if n in (0, GQ) and b < PAIRS - 1:
                    pe.wait_ge(o_loaded[n // GQ][b], 32)
                if n == ORDER[0] and b == PAIRS - 1:
                    pe.wait_ge(o_lo, 2 * PAIRS)
                if b == first:
                    if n == 0 and partial:
                        pe.wait_ge(stage_ready, 2 * UNITS0 + 8 * (PAIRS - 1) + 2)
                    elif partial or at == 0:
                        pe.wait_ge(partial_sum, n)
                    elif at < BANKS:
                        pe.wait_ge(beta_ready, SLOTS * PAIRS)
                    else:
                        pe.wait_ge(y_sum, at - BANKS + 1)
                bank = proj_ps if partial else y_banks[at % BANKS]
                for m, (ol, wl) in enumerate(((0, 0), (0, 1), (1, 0))):
                    mm = nc.tensor.matmul(bank[:, :], hT[:, ol, b, tokens], w_out_of(nh, wl)[:, b, :],
                                          start=(b == first and m == 0), stop=(b == last and m == 2))
                if partial and b == last:
                    mm.then_inc(partial_done, 1)
                return mm

            def scores(p, par, s):
                hh, i = s // 8, s % 8
                width = P * (i + 1)
                if s == 0:
                    pe.wait_ge(qk_split, 4 * p + 4)
                    pe.wait_ge(k_swapped, 64 * p + 64)
                    if is_first(p):
                        pe.wait_ge(xt_lo, 2 * KB)
                wait(pe, beta_ready, SLOTS * p + s - 1)
                z, q, first = z_ps[s % 2], q_of(par, hh)[:, i * P:(i + 1) * P], z_offset(i)
                for c in range(0, first + width, HALF):
                    c0, c1 = max(c, first), min(c + HALF, first + max(width, 2 * P))
                    for swapped in (False, True):
                        mm = nc.tensor.matmul(z[:, c0:c1], q, k_of(par, hh, swapped)[:, c0 - first:c1 - first],
                                              start=not swapped, stop=swapped)
                mm.then_inc(z_ready, 1)

            def project_part(p, s):
                half, b0, b1 = proj_part(p, s)
                unit = 0 if is_last(p) else s // 4
                if half == 0:
                    pe.wait_ge(w_ready, 2 * UNITS0 + 8 * p + 2 * unit + b0 // 4 + 1)
                if b0 == 0:
                    pe.wait_ge(stage_ready, 2 * UNITS0 + 8 * p + 2 * unit + half - (is_first(p) and s == 0))
                for b in range(b0, b1 + 1):
                    mm = project((UNITS0 + unit) % 2, proj_ps, half, b)
                if b1 == KB - 1:
                    mm.then_inc(proj_done, 1)

            def slot(p, par, s):
                q_late = is_first(p) and s == 0
                if q_late:
                    project_part(p, s)
                if not is_tail(p):
                    for block in {0: (s, s + 1), 1: ()}.get(s % 8, (s,)):
                        scores(p, par, block)
                if v_t_at(p, s) is not None:
                    t = v_t_at(p, s)
                    transpose_v(t_base(p) + t, t % 2, 2 * UNITS0 + 8 * p + 2 + (s == 8), int(s == 8))
                if not is_tail(p) and s in proj_slots(p) and not q_late:
                    project_part(p, s)
                if isinstance(p, int):
                    for _ in range(EARLY_BY_SLOT.get((p, s), 0)):
                        project_out(*early.pop(0))
                for t, av, ahh, grp, j in av_at(p, s):
                    apar = 1 - par if s < 5 else par
                    pe.wait_ge(t_lo, t_base(p) + t + 1)
                    if j == 0:
                        group = {1: -1, 5: 0, 9: 1, 13: 2}[s]
                        wait(pe, o_summed, 4 * p + group)
                    rel = max(0, j - GQ * grp)
                    for hl in range(2):
                        if rel == GQ - 1:
                            c, moving = HALF - 2 * P, aT_pad[:, hl, :]
                        else:
                            c = rel * P
                            moving = aT[:, av % 2, hl, c:HALF]
                        mm = nc.tensor.matmul(o_ps[:, c:HALF], v_of(apar)[:, j, 2 * ahh:2 * ahh + 2, :]
                                              .rearrange("p x d -> p (x d)"), moving,
                                              start=(j == 0 and hl == 0),
                                              stop=(j == GQ * (grp + 1) - 1 and hl == 1))
                    mm.then_inc(av_done, 1)
                for t, av, thh, grp, j in units_at(p, s):
                    wait(pe, t_lo, t_base(p) + t - 1)
                    if j == 0:
                        pe.wait_ge(a_ready, SLOTS * p + (0 if s < 4 else 4 * (s // 4)))
                    for i2 in range(max(0, j - GQ * grp), GQ):
                        last = nc.tensor.transpose(t_ps[t % 2][:, i2 * P:(i2 + 1) * P],
                                                   a_g[grp][:, i2, j * P:(j + 1) * P], ident[:, :])
                    last.then_inc(t_done, 1)

            over_pairs(pe, slot, 4)

            while early:
                project_out(*early.pop(0))
            for n in ORDER:
                for b in range(PAIRS - 1 if n in [*ORDER[:BANKS], *range(PARTIAL_TILES)] else 0, KB):
                    mm = project_out(n, b)
                mm.then_inc(y_done, 1)

        @block.scalar
        def _(act):
            for b in range(0, KB, 2):
                load_x_block(act, b)
            act.wait_ge(consts_ready, 4)

            def root(cols, ready, count):
                act.wait_ge(ready, count)
                nc.scalar.activation(rstd[:, cols], ssq[:, cols], ACT.Sqrt, scale=1.0 / D,
                                     bias=eps_col[:, :]).then_inc(root_ready, 1)

            nc.scalar.activation(newton[:, 0:1], eps_col[:, :], ACT.Sqrt).then_inc(table_loaded, 1)

            def square_x(n, b):
                act.wait_ge(x_loaded[b], 16)
                wait(act, x_squared, n)
                nc.scalar.activation(oT[:, :], x_blocks[b], ACT.Square,
                                     accum_out=ssq[:, b:b + 1]).then_inc(x_squared, 1)

            def hi_x(n):
                half, b = n // KB, n % KB
                act.wait_ge(xt_done, n + 1)
                nc.scalar.activation(hT[:, 0, b, half * HALF:(half + 1) * HALF], z_banks[n % 4][:, :],
                                     ACT.Copy, scale=g_col[:, b:b + 1]).then_inc(xt_hi, 1)

            square_x(0, 0)
            square_x(1, 2)
            act.wait_ge(x_squared_dve, 2)
            root(slice(0, 4), x_squared, 2)
            square_x(2, 4)

            def scale_x(blocks):
                for b in blocks:
                    nc.scalar.activation(x_blocks[b], x_blocks[b], ACT.Copy, scale=rstd[:, b:b + 1]
                                         ).then_inc(x_scaled_act, 1)

            act.wait_ge(rstd_ready, 5)
            scale_x(X_ACT[:1])
            act.wait_ge(g_loaded, 16)
            for n in range(KB):
                hi_x(n)
                if n in (3, 4):
                    square_x(n, n + 3)
                if n == 5:
                    act.wait_ge(x_squared_dve, 3)
                    root(slice(4, 8), x_squared, 5)
            act.wait_ge(rstd_ready, 10)
            scale_x(X_ACT[1:])

            def v_hi(par, half, t_index, t_bank):
                act.wait_ge(t_done, t_index + 1)
                nc.scalar.activation(v_of(par)[:, GQ * half:GQ * half + GQ, 0:4:3, :],
                                     t_ps[t_bank][:, :].rearrange("p (b x d) -> p b x d", b=GQ, x=2),
                                     ACT.Copy).then_inc(t_hi, 1)

            def to_stage(bank, h, buf):
                act.wait_ge(proj_done, h + 1)
                nc.scalar.activation(stage[:, buf, :], bank[:, :], ACT.Copy).then_inc(stage_ready, 1)

            for h, (kind, half) in enumerate(PROLOGUE):
                if h in (2, 4):
                    act.wait_ge(qk_split, h // 2)
                if h in (3, 5):
                    act.wait_ge(t_done, h // 2)
                to_stage((proj_ps, o_ps)[h % 2], h, h % 2)
                if h == 0:
                    for n in range(KB, 2 * KB):
                        hi_x(n)
                if h in (3, 5):
                    v_hi(0, h // 2 - 1, h // 2 - 1, h // 2 - 1)

            def slot(p, par, s):
                evac = evac_at(p, s)
                if evac:
                    kind, half, h = evac
                    if kind == "g" and (s == 0 or not is_last(p)):
                        act.wait_ge(qk_split, 4 * p + (4 if s == 0 else 7 + half))
                    elif kind == "v":
                        act.wait_ge(qk_split, 4 * p + 5 + half)
                    elif kind == "q":
                        act.wait_ge(t_done, t_base(p) + STEADY[8 if half else 6][0] + 1)
                    elif is_first(p):
                        act.wait_ge(qk_split, 3 + half)
                    else:
                        act.wait_ge(gate_ready, 2 * p - 1 + half)
                    to_stage(proj_ps, h, half)
                if gate_at(p, s):
                    half, number = gate_at(p, s)
                    act.wait_ge(stage_ready, evac[2] + 1)
                    wait(act, o_gated, number - 1)
                    nc.scalar.activation(gate[:, half * HALF:(half + 1) * HALF], stage[:, half, :],
                                         ACT.Sigmoid).then_inc(gate_sig, 1)
                if s % 4 == 1 and av_at(p, s - 1) and (not is_tail(p) or s < 9):
                    _, av, ohh, grp, _ = av_at(p, s - 1)[-1]
                    act.wait_ge(av_done, av_base(p) + av + 1)
                    if ohh == 0:
                        wait(act, o_lo, 2 * p - 1 + grp)
                    rows = slice(HD * ohh, HD * ohh + HD)
                    other = slice(HD - HD * ohh, 2 * HD - HD * ohh)
                    nc.scalar.activation(oT[rows, grp * HALF:(grp + 1) * HALF], o_ps[other, :],
                                         ACT.Copy).then_inc(o_shift, 1)
                for t, av, _, grp, j in (units_at(p, s - 1) if s else av_at(p, 0)):
                    rel = max(0, j - GQ * grp)
                    act.wait_ge(t_done, t_base(p) + t + 1)
                    wait(act, av_done, av_base(p) + av - 1)
                    to = aT_pad[:, 0, P:2 * P] if rel == GQ - 1 else aT[:, av % 2, 0, rel * P:HALF]
                    nc.scalar.activation(to, t_ps[t % 2][:, rel * P:HALF], ACT.Copy).then_inc(t_hi, 1)
                if s in (2, 6) and not is_first(p):
                    half = s // 4
                    act.wait_ge(o_gated, 2 * p - 1 + half)
                    if not is_tail(p):
                        wait(act, o_stored, 64 * (p - 1) + 32 * half)
                    nc.scalar.activation(split_of(p, half)[0], oT[:, half * HALF:(half + 1) * HALF],
                                         ACT.Copy).then_inc(o_hi, 1)
                if is_tail(p):
                    return
                hh, i = s // 8, s % 8
                width, grp, first = P * (i + 1), i // GQ, z_offset(i)
                act.wait_ge(z_ready, SLOTS * p + s + 1)
                wait(act, a_ready, SLOTS * p + s - 1)
                nc.scalar.activation(rest[:, s % 2, S - width:S], z_ps[s % 2][:, first:first + width], ACT.Sigmoid,
                                     scale=-SCALE).then_inc(rest_ready, 1)
                nc.scalar.activation(a_g[grp][:, i % GQ, 0:width], z_ps[s % 2][:, first:first + width],
                                     ACT.Sigmoid, scale=SCALE).then_inc(beta_ready, 1)
                if v_t_at(p, s) is not None:
                    t = v_t_at(p, s)
                    v_hi(1 - par, s // 8, t_base(p) + t, t % 2)
                if is_last(p):
                    for n in WO_BY_SLOT.get(s, ()):
                        wait_wo(act, n)
                        nc.scalar.activation(w_out_of(0, 0)[:, n, :], wo_raw[:, n % WO_RING, :], ACT.Copy
                                             ).then_inc(wo_hi, 1)

            over_pairs(act, slot)

            for at, n in enumerate(ORDER):
                act.wait_ge(y_sum, at + 1)
                wait(act, y_squared, at)
                nc.scalar.activation(rest[:, 0, 0:HALF], y_of(n), ACT.Square, accum_out=ssq[:, n:n + 1]
                                     ).then_inc(y_squared, 1)
                if n >= KB:
                    b = n - KB
                    root(slice(b, b + 1), ssq_summed, b + 1)
                    act.wait_ge(y_weighted, 2 * b + 1)
                    act.wait_ge(rstd_ready, 5 * (b + 3))
                    nc.scalar.activation(out_of(b)[0], out_of(b)[0], ACT.Copy, scale=rstd[:, b:b + 1]
                                         ).then_inc(out_ready_act, 1)
                    act.wait_ge(out_ready_act, b + 1)
                    act.dma_start(out[b * P:(b + 1) * P, 0:HALF], out_of(b)[0]).then_inc(stored[b % 2], 16)
                    if b < KB - 1:
                        act.wait_ge(out_ready, b + 1)
                        act.dma_start(out[b * P:(b + 1) * P, HALF:S], out_of(b)[1]).then_inc(stored[b % 2], 16)
            for odd in range(2):
                act.wait_ge(stored[odd], 16 * KB)

        @block.vector
        def _(dve):
            def split_hi_w(ring, part):
                nc.vector.tensor_copy(w_split[:, ring, 0, 4 * part:4 * part + 4, :],
                                      w_raw[:, part, :].rearrange("p (b n) -> p b n", b=4)).then_inc(w_hi, 1)

            def rsqrt(cols, n):
                r, m, t = rstd[:, cols], mean_sq[:, cols], newton[:, cols]
                nc.vector.tensor_scalar(m, ssq[:, cols], 1.0 / D, EPS, ALU.mult, ALU.add).then_inc(mean_ready, 1)
                dve.wait_ge(root_ready, n + 1)
                nc.vector.reciprocal(r, r).then_inc(rstd_ready, 1)
                dve.wait_ge(mean_ready, n + 1)
                dve.wait_ge(rstd_ready, 5 * n + 1)
                nc.vector.tensor_tensor(t, r, r, ALU.mult).then_inc(rstd_ready, 1)
                dve.wait_ge(rstd_ready, 5 * n + 2)
                nc.vector.tensor_tensor(t, t, m, ALU.mult).then_inc(rstd_ready, 1)
                dve.wait_ge(rstd_ready, 5 * n + 3)
                nc.vector.tensor_scalar(t, t, -0.5, 1.5, ALU.mult, ALU.add).then_inc(rstd_ready, 1)
                dve.wait_ge(rstd_ready, 5 * n + 4)
                nc.vector.tensor_tensor(r, r, t, ALU.mult).then_inc(rstd_ready, 1)
                dve.wait_ge(rstd_ready, 5 * n + 5)

            nc.vector.memset(aT_pad[:, :, 0:P].bitcast(F32), 0.0)
            nc.vector.memset(eps_col[:, :], EPS)
            nc.vector.memset(rest[:, :, S:S + 1], 1.0).then_inc(consts_ready, 1)
            def square_x(n, b):
                dve.wait_ge(x_loaded[b], 16)
                wait(dve, x_squared_dve, n)
                nc.vector.tensor_tensor_reduce(gate[:, :], x_blocks[b], x_blocks[b], 1.0, 0.0, ALU.mult, ALU.add,
                                               ssq[:, b:b + 1]).then_inc(x_squared_dve, 1)

            def scale_x(blocks):
                for b in blocks:
                    nc.vector.tensor_scalar(x_blocks[b], x_blocks[b], rstd[:, b:b + 1], None,
                                            ALU.mult).then_inc(x_scaled, 1)

            def lo_x(n):
                half, b = n // KB, n % KB
                cols = slice(half * HALF, (half + 1) * HALF)
                dve.wait_ge(xt_hi, n + 1)
                nc.vector.scalar_tensor_tensor(hT[:, 1, b, cols], z_banks[n % 4][:, :], g_col[:, b:b + 1],
                                               hT[:, 0, b, cols].bitcast(F32), ALU.mult, ALU.subtract
                                               ).then_inc(xt_lo, 1)

            def next_w(n):
                dve.wait_ge(w_loaded[n % 2], 16 * (n // 2 + 1))
                split_hi_w((n // 2) % 2, n % 2)

            square_x(0, 1)
            square_x(1, 3)
            dve.wait_ge(table_loaded, 1)
            dve.wait_ge(x_squared_dve, 2)
            dve.wait_ge(x_squared, 2)
            rsqrt(slice(0, 4), 0)
            scale_x(X_DVE[:3])
            next_w(0)
            next_w(1)
            dve.wait_ge(g_loaded, 16)
            for n in range(KB):
                lo_x(n)
                if n == 2:
                    square_x(2, 5)
                    next_w(2)
                if n == 3:
                    next_w(3)
                if n == 6:
                    dve.wait_ge(x_squared, 5)
                    dve.wait_ge(x_squared_dve, 3)
                    rsqrt(slice(4, 8), 1)
            scale_x(X_DVE[3:])

            def split_heads(kind, par, half, h, buf, count):
                dve.wait_ge(stage_ready, h + 1)
                cols = slice(half * HALF, (half + 1) * HALF)
                for hh in range(2):
                    rows = slice(HD * hh, HD * hh + HD)
                    to = q_of(par, hh) if kind == "q" else k_of(par, hh, False)
                    last = nc.vector.tensor_copy(to[rows, cols], stage[rows, buf, :])
                last.then_inc(qk_hi, 1)
                dve.wait_ge(qk_hi, count)
                for hh in range(2):
                    rows = slice(HD * hh, HD * hh + HD)
                    other = slice(HD - HD * hh, 2 * HD - HD * hh)
                    to = q_of(par, hh) if kind == "q" else k_of(par, hh, False)
                    last = nc.vector.tensor_tensor(to[other, cols], stage[rows, buf, :],
                                                   to[rows, cols].bitcast(F32), ALU.subtract)
                last.then_inc(qk_split, 1)

            def v_lo(par, half, t_index, t_bank):
                dve.wait_ge(t_hi, t_index + 1)
                blocks = slice(GQ * half, GQ * half + GQ)
                nc.vector.tensor_tensor(v_of(par)[:, blocks, 1:3, :],
                                        t_ps[t_bank][:, :].rearrange("p (b x d) -> p b x d", b=GQ, x=2),
                                        v_of(par)[:, blocks, 0:4:3, :].bitcast(F32), ALU.subtract
                                        ).then_inc(t_lo, 1)

            for n in range(KB, 2 * KB):
                lo_x(n)
                if n == KB + 2:
                    split_heads("k", 0, 0, 0, 0, 1)
            for h, (kind, half) in enumerate(PROLOGUE):
                if h in (2, 4, 5):
                    split_heads(kind, 0, half, h, h % 2, {2: 2, 4: 3, 5: 4}[h])
                if h in (3, 5):
                    v_lo(0, h // 2 - 1, h // 2 - 1, h // 2 - 1)
                if h in (2, 3):
                    dve.wait_ge(proj_done, h + 1)
                    next_w(2 * h)
                    next_w(2 * h + 1)

            def wo_hi_part(n):
                wait_wo(dve, n)
                nc.vector.tensor_copy(w_out_of(n // KB, 0)[:, n % KB, :], wo_raw[:, n % WO_RING, :]
                                      ).then_inc(wo_hi, 1)

            def slot(p, par, s):
                evac = evac_at(p, s)
                if evac:
                    kind, half, h = evac
                    if kind in "kq":
                        split_heads(kind, 1 - par, half, h, half,
                                    4 * p + 5 + half + (2 if kind == "q" else 0))
                if gate_at(p, s):
                    half, number = gate_at(p, s)
                    dve.wait_ge(gate_sig, number + 1)
                    cols = slice(half * HALF, (half + 1) * HALF)
                    nc.vector.tensor_tensor(gate[:, cols], stage[:, half, :], gate[:, cols], ALU.mult
                                            ).then_inc(gate_ready, 1)
                if s % 4 == 1 and av_at(p, s - 1) and (not is_tail(p) or s < 9):
                    _, _, ohh, grp, _ = av_at(p, s - 1)[-1]
                    group = {1: -1, 5: 0, 9: 1, 13: 2}[s]
                    dve.wait_ge(o_shift, 4 * p + group)
                    rows = slice(HD * ohh, HD * ohh + HD)
                    cols = slice(grp * HALF, (grp + 1) * HALF)
                    nc.vector.tensor_tensor(oT[rows, cols], o_ps[rows, :], oT[rows, cols], ALU.add
                                            ).then_inc(o_summed, 1)
                for t, av, _, grp, j in (units_at(p, s - 1) if s else av_at(p, 0)):
                    rel = max(0, j - GQ * grp)
                    dve.wait_ge(t_hi, t_base(p) + t + 1)
                    if rel == GQ - 1:
                        hi, lo = aT_pad[:, 0, P:2 * P], aT_pad[:, 1, P:2 * P]
                    else:
                        hi, lo = aT[:, av % 2, 0, rel * P:HALF], aT[:, av % 2, 1, rel * P:HALF]
                    nc.vector.tensor_tensor(lo, t_ps[t % 2][:, rel * P:HALF], hi.bitcast(F32), ALU.subtract
                                            ).then_inc(t_lo, 1)
                if s in (2, 6) and not is_first(p):
                    half = s // 4
                    dve.wait_ge(o_hi, 2 * p - 1 + half)
                    hi, lo = split_of(p, half)
                    nc.vector.tensor_tensor(lo, oT[:, half * HALF:(half + 1) * HALF], hi.bitcast(F32),
                                            ALU.subtract).then_inc(o_lo, 1)
                if is_tail(p):
                    return
                width = P * (s % 8 + 1)
                span = rest[:, s % 2, S - 1:(S - 1 - width if width < S else None):-1]
                if is_first(p) and s == 0:
                    dve.wait_ge(consts_ready, 4)
                dve.wait_ge(rest_ready, SLOTS * p + s + 1)
                diagonal = rest[:, s % 2, S - P:S]
                nc.vector.tensor_tensor(diagonal, diagonal, not_before[:, :], ALU.max).then_inc(rest_masked, 1)
                dve.wait_ge(rest_masked, SLOTS * p + s + 1)
                nc.vector.tensor_tensor_scan(span, span, span, 1.0, ALU.mult, ALU.bypass
                                             ).then_inc(scan_done, 1)
                if v_t_at(p, s) is not None:
                    t = v_t_at(p, s)
                    v_lo(1 - par, s // 8, t_base(p) + t, t % 2)
                if s % 4 in (1, 2) and not is_last(p):
                    part = s % 4 - 1
                    unit = UNITS0 + 4 * p + s // 4 + 1
                    dve.wait_ge(proj_done, 2 * unit - 2)
                    dve.wait_ge(w_loaded[part], 16 * unit + 16)
                    split_hi_w((UNITS0 + 1 + s // 4) % 2, part)
                if is_last(p):
                    for n in WO_BY_SLOT.get(s, ()):
                        dve.wait_ge(wo_hi, n + 1)
                        wo_lo_part(nc.vector, n)
                if is_last(p) and s in PARTIAL_SLOTS:
                    n = PARTIAL_SLOTS.index(s)
                    dve.wait_ge(partial_done, n + 1)
                    dve.wait_ge(xs_loaded[n], 16)
                    nc.vector.tensor_tensor(stage[:, n, :], proj_ps[:, :], stage[:, n, :], ALU.add
                                            ).then_inc(partial_sum, 1)

            over_pairs(dve, slot)

            def weigh(b, half):
                nc.vector.tensor_tensor(out_of(b)[half], y_of(b + KB * half),
                                        rest[:, 1, half * HALF:(half + 1) * HALF], ALU.mult
                                        ).then_inc(y_weighted, 1)

            for at, n in enumerate(ORDER):
                b = n % KB
                for block in WO_BY_TILE.get(at, ()):
                    wo_hi_part(KB + block)
                if n >= KB:
                    if b == 0:
                        dve.wait_ge(fg_loaded, 16)
                    wait(dve, stored[b % 2], 32 * (b // 2))
                    dve.wait_ge(y_sum, at)
                    weigh(b, 0)
                dve.wait_ge(y_done, at + 1)
                if n < PARTIAL_TILES:
                    addend = stage[:, n, :]
                else:
                    dve.wait_ge(xr_loaded[at % 4], 16 * X_COUNT[at])
                    addend = a_g[0][:, at % 4, :]
                if n >= KB:
                    wait(dve, y_squared, n - 1)
                nc.vector.tensor_tensor(y_of(n), y_banks[at % BANKS][:, :], addend, ALU.add
                                        ).then_inc(y_sum, 1)
                if n < KB:
                    continue
                dve.wait_ge(y_sum, at + 1)
                weigh(b, 1)
                dve.wait_ge(y_squared, n + 1)
                nc.vector.tensor_tensor(ssq[:, b:b + 1], ssq[:, b:b + 1], ssq[:, n:n + 1], ALU.add
                                        ).then_inc(ssq_summed, 1)
                dve.wait_ge(ssq_summed, b + 1)
                rsqrt(slice(b, b + 1), 2 + b)
                dve.wait_ge(y_weighted, 2 * b + 2)
                nc.vector.tensor_scalar(out_of(b)[1], out_of(b)[1], rstd[:, b:b + 1], None,
                                        ALU.mult).then_inc(out_ready, 1)

        @block.gpsimd
        def _(pool):
            pool.dma_start(g_col[:, :], norm_g).then_inc(g_loaded, 16)
            for table, value in ((ident, 0.0), (before, 1.0), (not_before, 0.0)):
                last = nc.gpsimd.memset(table[:, :], value)
            last.then_inc(zeros_ready, 1)
            pool.wait_ge(zeros_ready, 1)
            for table, keep, fill in ((ident, ALU.not_equal, 1.0), (before, ALU.is_gt, 0.0),
                                      (not_before, ALU.is_gt, 1.0)):
                nc.gpsimd.affine_select(out=table[:, :], in_=table[:, :], compare_op=keep, fill=fill, base=0,
                                        pattern=[[-1, P]], channel_multiplier=1).then_inc(consts_ready, 1)

            def lo_w(n, ring, part):
                pool.wait_ge(w_hi, n + 1)
                to = w_split[:, ring, :, 4 * part:4 * part + 4, :]
                nc.gpsimd.tensor_tensor(to[:, 1], w_raw[:, part, :].rearrange("p (b n) -> p b n", b=4),
                                        to[:, 0].bitcast(F32), ALU.subtract).then_inc(w_ready, 1)

            for n in range(2 * UNITS0 + 2):
                lo_w(n, (n // 2) % 2, n % 2)

            def slot(p, par, s):
                if s in (1, 5) and not is_first(p):
                    half = s // 4
                    pool.wait_ge(o_summed, 4 * p - 1 + half)
                    pool.wait_ge(gate_ready, 2 * p - 1 + half)
                    cols = slice(half * HALF, (half + 1) * HALF)
                    nc.gpsimd.tensor_tensor(oT[:, cols], oT[:, cols], gate[:, cols], ALU.mult
                                            ).then_inc(o_gated, 1)
                if is_tail(p):
                    return
                i = s % 8
                width = P * (i + 1)
                a = a_g[i // GQ][:, i % GQ, 0:width]
                if is_first(p) and s == 0:
                    pool.wait_ge(consts_ready, 4)
                pool.wait_ge(beta_ready, SLOTS * p + s + 1)
                diagonal = a[:, width - P:width]
                nc.gpsimd.tensor_tensor(diagonal, diagonal, before[:, :], ALU.mult).then_inc(beta_masked, 1)
                pool.wait_ge(beta_masked, SLOTS * p + s + 1)
                pool.wait_ge(scan_done, SLOTS * p + s + 1)
                nc.gpsimd.tensor_tensor(a, a, rest[:, s % 2, S + 1 - width:S + 1], ALU.mult
                                        ).then_inc(a_ready, 1)
                if s % 4 in (1, 2) and not is_last(p):
                    n = 2 * (UNITS0 + 4 * p + s // 4 + 1) + s % 4 - 1
                    lo_w(n, (UNITS0 + 1 + s // 4) % 2, s % 4 - 1)

            over_pairs(pool, slot)

            for n in range(KB, 2 * KB):
                pool.wait_ge(wo_hi, n + 1)
                wo_lo_part(nc.gpsimd, n)


def kernel(**inputs):
    import numpy as _np
    import concourse.bacc as _bacc
    from concourse.bass_utils import run_bass_kernel_spmd as _run

    nc = _bacc.Bacc("TRN2", target_bir_lowering=False, num_devices=1)
    arrays = {
        "x": inputs["x"].reshape(S, D),
        "norm_g": inputs["norm_g"].reshape(KB, P).T,
        "w_in": inputs["sb_w_in"].reshape(2, GQ, P, 4 * KB, P).transpose(3, 0, 2, 1, 4)
                                 .reshape(4 * KB, 2, P, HALF),
        "w_out": inputs["sb_w_out"].reshape(D, D),
        "final_g": inputs["final_g"].reshape(D),
    }
    arrays = {name: _np.ascontiguousarray(a) for name, a in arrays.items()}
    aps = {name: nc.dram_tensor(name, a.shape, F32, kind="ExternalInput").ap() for name, a in arrays.items()}
    out = nc.dram_tensor("out", [S, D], F32, kind="ExternalOutput").ap()
    stick_breaking_layer(nc, aps["x"], aps["norm_g"], aps["w_in"], aps["w_out"], aps["final_g"], out)
    r = _run(nc, [arrays], core_ids=[0])
    return r.results[0]["out"].reshape(1, S, D)
```
